# Optimizing a Trainium2 kernel written in Bass

```python
import math, functools
import jax, jax.numpy as jnp
from jax import lax
import numpy as np

D_MODEL = 2048
BATCH = 1
SEQ = 256
DEPTH = 1

GRID_W = 64
CTX_LEN = 256
N_MIXERS = 2
S5_GROUP = 16
S5_GROUPS = D_MODEL // S5_GROUP
S5_STATE = 64
S5_DT_MIN = 0.001
S5_DT_MAX = 0.1
HG_HEADS = 16
HG_DK = D_MODEL // HG_HEADS
HG_DV = D_MODEL // HG_HEADS
HG_CHUNK = 32
MLP_HIDDEN = 4 * D_MODEL
NORM_EPS = 1e-6


def rmsnorm(x, g):
    xf = x.astype(jnp.float32)
    y = xf * lax.rsqrt(jnp.mean(xf * xf, axis=-1, keepdims=True) + NORM_EPS)
    return (y * g.astype(jnp.float32)).astype(x.dtype)

def adaln(cond, w, b):
    return jnp.split(jax.nn.silu(cond) @ w + b, 6, axis=-1)

def modulate(h, shift, scale):
    return h * (1 + scale) + shift

def raster_to_colmajor(h):
    b, n, d = h.shape
    rows = n // GRID_W
    return h.reshape(b, rows, GRID_W, d).transpose(0, 2, 1, 3).reshape(b, n, d)

def colmajor_to_raster(h):
    b, n, d = h.shape
    rows = n // GRID_W
    return h.reshape(b, GRID_W, rows, d).transpose(0, 2, 1, 3).reshape(b, n, d)

def sq_relu_mlp(h, w1, w2):
    return jnp.square(jax.nn.relu(h @ w1)) @ w2

def s5_discretise(a_re, a_im, log_dt, b_re, b_im):
    lam = lax.complex(a_re.astype(jnp.float32), a_im.astype(jnp.float32))
    dt = jnp.exp(log_dt.astype(jnp.float32))[:, None]
    lam_bar = jnp.exp(lam * dt)
    b = lax.complex(b_re.astype(jnp.float32), b_im.astype(jnp.float32))
    b_bar = ((lam_bar - 1) / lam)[..., None] * b
    return lam_bar, b_bar

def _lin_rec_combine(e1, e2):
    a1, b1 = e1
    a2, b2 = e2
    return a1 * a2, a2 * b1 + b2

def s5_scan(u, lam_bar, b_bar, s0, reverse):
    bu = jnp.einsum('btgh,gph->btgp', u, b_bar)
    first = -1 if reverse else 0
    bu = bu.at[:, first].add(lam_bar * s0)
    a = jnp.broadcast_to(lam_bar, bu.shape)
    _, states = lax.associative_scan(_lin_rec_combine, (a, bu), axis=1, reverse=reverse)
    return states

def s5_mixer(h_ctx, h_lat, a_re, a_im, log_dt, b_re, b_im, c_re, c_im, d_skip, w_glu, ctx_out):
    def to_groups(h):
        return h.astype(jnp.float32).reshape(h.shape[0], h.shape[1], S5_GROUPS, S5_GROUP)

    u_ctx, u_lat = to_groups(h_ctx), to_groups(h_lat)
    uc_ctx, uc_lat = u_ctx.astype(jnp.complex64), u_lat.astype(jnp.complex64)
    d = d_skip.astype(jnp.float32).reshape(S5_GROUPS, S5_GROUP)
    y_lat = u_lat * d
    y_ctx = u_ctx * d if ctx_out else None
    s0 = jnp.zeros((h_lat.shape[0], S5_GROUPS, S5_STATE), jnp.complex64)
    for direction in range(2):
        reverse = direction == 1
        lam_bar, b_bar = s5_discretise(a_re[direction], a_im[direction], log_dt[direction],
                                       b_re[direction], b_im[direction])
        c_mat = lax.complex(c_re[direction].astype(jnp.float32), c_im[direction].astype(jnp.float32))
        st_ctx = s5_scan(uc_ctx, lam_bar, b_bar, s0, reverse)
        s_ctx_final = st_ctx[:, 0] if reverse else st_ctx[:, -1]
        st_lat = s5_scan(uc_lat, lam_bar, b_bar, s_ctx_final, reverse)
        y_lat = y_lat + jnp.einsum('btgp,ghp->btgh', st_lat, c_mat).real
        if ctx_out:
            y_ctx = y_ctx + jnp.einsum('btgp,ghp->btgh', st_ctx, c_mat).real

    def glu_out(y, h):
        z = jax.nn.gelu(y.reshape(h.shape).astype(h.dtype))
        a, g = jnp.split(z @ w_glu, 2, axis=-1)
        return a * jax.nn.sigmoid(g)

    return (glu_out(y_ctx, h_ctx) if ctx_out else None), glu_out(y_lat, h_lat)

def hgrn_project(h, w_in, with_query):
    def heads(t):
        return t.astype(jnp.float32).reshape(t.shape[0], t.shape[1], HG_HEADS, -1)
    if with_query:
        q, i, zf, zb, g = jnp.split(h @ w_in, 5, axis=-1)
        return heads(jax.nn.silu(q)), heads(i), heads(zf), heads(zb), g
    i, zf, zb = jnp.split(h @ w_in[:, D_MODEL:4 * D_MODEL], 3, axis=-1)
    return None, heads(i), heads(zf), heads(zb), None

def forget_gate(logit, lb):
    lb = lb.astype(jnp.float32).reshape(HG_HEADS, HG_DK)
    log_f = jnp.logaddexp(jax.nn.log_sigmoid(logit), jnp.log(lb) + jax.nn.log_sigmoid(-logit))
    k = (1 - lb) * jax.nn.sigmoid(-logit)
    return log_f, k

def chunked_gated_recurrence(q, k, v, logf, s0):
    b_, t, h, kd = k.shape
    n = t // HG_CHUNK

    def chunks(z):
        return z.reshape(b_, n, HG_CHUNK, h, z.shape[-1])

    k, v, logf = chunks(k), chunks(v), chunks(logf)
    cum = jnp.cumsum(logf, axis=2)
    cum_last = cum[:, :, -1]
    k_end = k * jnp.exp(cum_last[:, :, None] - cum)
    u = jnp.einsum('bnchk,bnchv->bnhkv', k_end, v)

    def step(s, inp):
        decay, inc = inp
        return decay[..., None] * s + inc, s

    s_fin, s_in = lax.scan(step, s0, (jnp.moveaxis(jnp.exp(cum_last), 1, 0), jnp.moveaxis(u, 1, 0)))
    if q is None:
        return None, s_fin
    s_in = jnp.moveaxis(s_in, 0, 1)
    q = chunks(q)
    qb = q * jnp.exp(cum)
    kb = k * jnp.exp(-cum)
    scores = jnp.einsum('bnchk,bnshk->bnhcs', qb, kb)
    mask = jnp.tril(jnp.ones((HG_CHUNK, HG_CHUNK), dtype=bool))
    scores = jnp.where(mask, scores, 0.0)
    o = jnp.einsum('bnhcs,bnshv->bnchv', scores, v) + jnp.einsum('bnchk,bnhkv->bnchv', qb, s_in)
    return o.reshape(b_, t, h, v.shape[-1]), s_fin

def hgrn_readout(o, g, o_norm, w_out):
    b_, t, h, dv = o.shape
    o = o * lax.rsqrt(jnp.mean(o * o, axis=-1, keepdims=True) + NORM_EPS)
    o = o.reshape(b_, t, h * dv) * o_norm.astype(jnp.float32)
    return (o.astype(g.dtype) * jax.nn.silu(g)) @ w_out

def hgrn_mixer(h_ctx, h_lat, w_in, lb_fwd, lb_bwd, o_norm, w_out, ctx_out):
    q_l, v_l, zf_l, zb_l, g_l = hgrn_project(h_lat, w_in, True)
    q_c, v_c, zf_c, zb_c, g_c = hgrn_project(h_ctx, w_in, ctx_out)
    s0 = jnp.zeros((h_lat.shape[0], HG_HEADS, HG_DK, HG_DV), jnp.float32)
    flip = functools.partial(jnp.flip, axis=1)
    o_lat, o_ctx = [], []
    for z_c, z_l, lb, reverse in ((zf_c, zf_l, lb_fwd, False), (zb_c, zb_l, lb_bwd, True)):
        orient = flip if reverse else (lambda z: z)
        logf_c, k_c = forget_gate(z_c, lb)
        logf_l, k_l = forget_gate(z_l, lb)
        oc, s_ctx = chunked_gated_recurrence(orient(q_c) if ctx_out else None, orient(k_c), orient(v_c),
                                             orient(logf_c), s0)
        ol, _ = chunked_gated_recurrence(orient(q_l), orient(k_l), orient(v_l), orient(logf_l), s_ctx)
        o_lat.append(orient(ol))
        if ctx_out:
            o_ctx.append(orient(oc))
    y_lat = hgrn_readout(o_lat[0] + o_lat[1], g_l, o_norm, w_out)
    y_ctx = hgrn_readout(o_ctx[0] + o_ctx[1], g_c, o_norm, w_out) if ctx_out else None
    return y_ctx, y_lat

def first_inputs(seed: int = 0) -> dict:
    key = jax.random.key(seed)
    ks = iter(jax.random.split(key, 32))
    d = D_MODEL
    n_s5 = (DEPTH + N_MIXERS - 1) // N_MIXERS
    n_hg = DEPTH // N_MIXERS
    f32 = jnp.float32

    def nrm(shape, scale):
        return scale * jax.random.normal(next(ks), shape, f32)

    def gain(shape):
        return 1.0 + 0.05 * jax.random.normal(next(ks), shape, f32)

    return {
        "x": nrm((BATCH, SEQ, d), 1.0),
        "c": nrm((BATCH, d), 1.0),
        "ctx": nrm((BATCH, CTX_LEN, d), 1.0),
        "c_ctx": nrm((d,), 1.0),
        "w_mod": nrm((DEPTH, d, 6 * d), 0.5 * d ** -0.5),
        "b_mod": nrm((DEPTH, 6 * d), 0.02),
        "norm_mix_pre": gain((DEPTH, d)),
        "norm_mix_post": gain((DEPTH, d)),
        "norm_mlp_pre": gain((DEPTH, d)),
        "norm_mlp_post": gain((DEPTH, d)),
        "w_mlp_in": nrm((DEPTH, d, MLP_HIDDEN), d ** -0.5),
        "w_mlp_out": nrm((DEPTH, MLP_HIDDEN, d), MLP_HIDDEN ** -0.5),
        "s5_a_re": -0.5 + nrm((n_s5, 2, S5_GROUPS, S5_STATE), 0.01),
        "s5_a_im": math.pi * jnp.arange(S5_STATE, dtype=f32) + nrm((n_s5, 2, S5_GROUPS, S5_STATE), 0.01),
        "s5_log_dt": jax.random.uniform(next(ks), (n_s5, 2, S5_GROUPS), f32,
                                        math.log(S5_DT_MIN), math.log(S5_DT_MAX)),
        "s5_b_re": nrm((n_s5, 2, S5_GROUPS, S5_STATE, S5_GROUP), (2 * S5_GROUP) ** -0.5),
        "s5_b_im": nrm((n_s5, 2, S5_GROUPS, S5_STATE, S5_GROUP), (2 * S5_GROUP) ** -0.5),
        "s5_c_re": nrm((n_s5, 2, S5_GROUPS, S5_GROUP, S5_STATE), S5_STATE ** -0.5),
        "s5_c_im": nrm((n_s5, 2, S5_GROUPS, S5_GROUP, S5_STATE), S5_STATE ** -0.5),
        "s5_d": nrm((n_s5, d), 1.0),
        "s5_w_glu": nrm((n_s5, d, 2 * d), d ** -0.5),
        "hg_w_in": nrm((n_hg, d, 5 * d), d ** -0.5),
        "hg_lb_raw": nrm((2, n_hg, HG_HEADS * HG_DK), 0.1),
        "hg_o_norm": gain((n_hg, d)),
        "hg_w_out": nrm((n_hg, d, d), d ** -0.5),
    }

def first_block(x, c, ctx, c_ctx, w_mod, b_mod, norm_mix_pre, norm_mix_post, norm_mlp_pre, norm_mlp_post,
              w_mlp_in, w_mlp_out, s5_a_re, s5_a_im, s5_log_dt, s5_b_re, s5_b_im, s5_c_re, s5_c_im, s5_d,
              s5_w_glu, hg_w_in, hg_lb_raw, hg_o_norm, hg_w_out):
    lb_w = jax.nn.softmax(hg_lb_raw.astype(jnp.float32), axis=1)
    lb = jnp.cumsum(lb_w, axis=1) - lb_w[:, :1]
    x_lat, x_ctx = x, ctx
    for layer in range(DEPTH):
        ctx_live = layer < DEPTH - 1
        j = layer // N_MIXERS
        sh1, sc1, gt1, sh2, sc2, gt2 = adaln(c, w_mod[layer], b_mod[layer])
        csh1, csc1, cgt1, csh2, csc2, cgt2 = adaln(c_ctx, w_mod[layer], b_mod[layer])
        h_lat = modulate(rmsnorm(x_lat, norm_mix_pre[layer]), sh1[:, None], sc1[:, None])
        h_ctx = modulate(rmsnorm(x_ctx, norm_mix_pre[layer]), csh1, csc1)
        if layer % N_MIXERS == 0:
            y_ctx, y_lat = s5_mixer(h_ctx, h_lat, s5_a_re[j], s5_a_im[j], s5_log_dt[j], s5_b_re[j], s5_b_im[j],
                                    s5_c_re[j], s5_c_im[j], s5_d[j], s5_w_glu[j], ctx_live)
        else:
            y_ctx, y_lat = hgrn_mixer(h_ctx, raster_to_colmajor(h_lat), hg_w_in[j], lb[0, j], lb[1, j],
                                      hg_o_norm[j], hg_w_out[j], ctx_live)
            y_lat = colmajor_to_raster(y_lat)
        x_lat = x_lat + gt1[:, None] * rmsnorm(y_lat, norm_mix_post[layer])
        h_lat = modulate(rmsnorm(x_lat, norm_mlp_pre[layer]), sh2[:, None], sc2[:, None])
        x_lat = x_lat + gt2[:, None] * rmsnorm(sq_relu_mlp(h_lat, w_mlp_in[layer], w_mlp_out[layer]),
                                               norm_mlp_post[layer])
        if ctx_live:
            x_ctx = x_ctx + cgt1 * rmsnorm(y_ctx, norm_mix_post[layer])
            h_ctx = modulate(rmsnorm(x_ctx, norm_mlp_pre[layer]), csh2, csc2)
            x_ctx = x_ctx + cgt2 * rmsnorm(sq_relu_mlp(h_ctx, w_mlp_in[layer], w_mlp_out[layer]),
                                           norm_mlp_post[layer])
    return x_lat


DEPTH_2 = 2

CONV_DIM = D_MODEL // 2
CONV_GROUPS = 8
CONV_GROUP_DIM = CONV_DIM // CONV_GROUPS
CONV_WIDTH = 31
CONV_PAD = (CONV_WIDTH - 1) // 2
SGU_DIM = D_MODEL // 2
SGU_HEADS = 8
SGU_HEAD_DIM = SGU_DIM // SGU_HEADS
CHUNK = 128
IN_DIM = 2 * CONV_DIM + 2 * SGU_DIM
MIX_DIM = CONV_DIM + SGU_DIM
FNET_GROUPS = 8
FNET_GROUP_DIM = D_MODEL // FNET_GROUPS
D_FF = ((8 * D_MODEL + 3 * 256 - 1) // (3 * 256)) * 256
N_EVEN = (DEPTH_2 + 1) // 2
N_ODD = DEPTH_2 // 2
RMS_EPS = 1e-6
LN_EPS = 1e-5


def rms_norm(x, g):
    xf = x.astype(jnp.float32)
    y = xf * lax.rsqrt(jnp.mean(xf * xf, axis=-1, keepdims=True) + RMS_EPS)
    return (y * g.astype(jnp.float32)).astype(x.dtype)

def layer_norm(x, g, b):
    xf = x.astype(jnp.float32)
    mu = jnp.mean(xf, axis=-1, keepdims=True)
    xc = xf - mu
    y = xc * lax.rsqrt(jnp.mean(xc * xc, axis=-1, keepdims=True) + LN_EPS)
    return (y * g.astype(jnp.float32) + b.astype(jnp.float32)).astype(x.dtype)

def conv_module(z, dw_w, dw_b, ln_g, ln_b):
    a, gate = jnp.split(z, 2, axis=-1)
    y = a * jax.nn.sigmoid(gate)
    y = lax.conv_general_dilated(
        y, dw_w[:, None, :], window_strides=(1,),
        padding=[(CONV_PAD, CONV_PAD)],
        dimension_numbers=("NWC", "WIO", "NWC"),
        feature_group_count=CONV_DIM) + dw_b
    b, s, _ = y.shape
    y = layer_norm(y.reshape(b, s, CONV_GROUPS, CONV_GROUP_DIM),
                   ln_g.reshape(CONV_GROUPS, CONV_GROUP_DIM),
                   ln_b.reshape(CONV_GROUPS, CONV_GROUP_DIM)).reshape(b, s, CONV_DIM)
    return jax.nn.silu(y)

def spatial_gating(z, ln_g, ln_b, w_s, b_s):
    z = jax.nn.gelu(z, approximate=False)
    u, v = jnp.split(z, 2, axis=-1)
    v = layer_norm(v, ln_g, ln_b)
    b, s, _ = v.shape
    v = v.reshape(b, s // CHUNK, CHUNK, SGU_HEADS, SGU_HEAD_DIM)
    mixed = jnp.einsum("hpq,bnqhc->bnphc", w_s, v) + b_s.T[None, None, :, :, None]
    return u * mixed.reshape(b, s, SGU_DIM)

def fourier_mix(h):
    b, s, d = h.shape
    hg = h.astype(jnp.float32).reshape(b, s, FNET_GROUPS, FNET_GROUP_DIM)
    y = jnp.fft.fft2(hg, axes=(1, 3), norm="ortho").real
    return y.reshape(b, s, d).astype(h.dtype)

def swiglu(h, w_gate, w_up, w_down):
    return (jax.nn.silu(h @ w_gate) * (h @ w_up)) @ w_down

def second_inputs(seed: int = 0) -> dict:
    key = jax.random.key(seed)
    ks = jax.random.split(key, 24)
    f32 = jnp.float32

    def nrm(k, shape, scale):
        return jax.random.normal(k, shape, f32) * scale

    def gain(k, shape):
        return 1.0 + 0.02 * jax.random.normal(k, shape, f32)

    return {
        "x": jax.random.normal(ks[0], (BATCH, SEQ, D_MODEL), f32),
        "mix_norm_g": gain(ks[1], (DEPTH_2, D_MODEL)),
        "ffn_norm_g": gain(ks[2], (DEPTH_2, D_MODEL)),
        "final_norm_g": gain(ks[3], (D_MODEL,)),
        "ab_w_in": nrm(ks[4], (N_EVEN, D_MODEL, IN_DIM), D_MODEL ** -0.5),
        "conv_dw_w": nrm(ks[5], (N_EVEN, CONV_WIDTH, CONV_DIM), CONV_WIDTH ** -0.5),
        "conv_dw_b": nrm(ks[6], (N_EVEN, CONV_DIM), 0.02),
        "conv_ln_g": gain(ks[7], (N_EVEN, CONV_DIM)),
        "conv_ln_b": nrm(ks[8], (N_EVEN, CONV_DIM), 0.02),
        "sgu_ln_g": gain(ks[9], (N_EVEN, SGU_DIM)),
        "sgu_ln_b": nrm(ks[10], (N_EVEN, SGU_DIM), 0.02),
        "sgu_w": nrm(ks[11], (N_EVEN, SGU_HEADS, CHUNK, CHUNK), CHUNK ** -0.5),
        "sgu_b": 1.0 + nrm(ks[12], (N_EVEN, SGU_HEADS, CHUNK), 0.01),
        "ab_w_out": nrm(ks[13], (N_EVEN, MIX_DIM, D_MODEL), MIX_DIM ** -0.5),
        "fnet_w_out": nrm(ks[14], (N_ODD, D_MODEL, D_MODEL), D_MODEL ** -0.5),
        "fnet_b_out": nrm(ks[15], (N_ODD, D_MODEL), 0.02),
        "ffn_w_gate": nrm(ks[16], (DEPTH_2, D_MODEL, D_FF), D_MODEL ** -0.5),
        "ffn_w_up": nrm(ks[17], (DEPTH_2, D_MODEL, D_FF), D_MODEL ** -0.5),
        "ffn_w_down": nrm(ks[18], (DEPTH_2, D_FF, D_MODEL), D_FF ** -0.5),
    }

def second_block(x, mix_norm_g, ffn_norm_g, final_norm_g, ab_w_in, conv_dw_w,
              conv_dw_b, conv_ln_g, conv_ln_b, sgu_ln_g, sgu_ln_b, sgu_w, sgu_b,
              ab_w_out, fnet_w_out, fnet_b_out, ffn_w_gate, ffn_w_up, ffn_w_down):
    for layer in range(DEPTH_2):
        h = rms_norm(x, mix_norm_g[layer])
        if layer % 2 == 0:
            i = layer // 2
            z = h @ ab_w_in[i]
            z_conv = z[..., : 2 * CONV_DIM]
            z_sgu = z[..., 2 * CONV_DIM:]
            y_conv = conv_module(z_conv, conv_dw_w[i], conv_dw_b[i],
                                 conv_ln_g[i], conv_ln_b[i])
            y_sgu = spatial_gating(z_sgu, sgu_ln_g[i], sgu_ln_b[i],
                                   sgu_w[i], sgu_b[i])
            x = x + jnp.concatenate([y_conv, y_sgu], axis=-1) @ ab_w_out[i]
        else:
            j = layer // 2
            x = x + fourier_mix(h) @ fnet_w_out[j] + fnet_b_out[j]
        h = rms_norm(x, ffn_norm_g[layer])
        x = x + swiglu(h, ffn_w_gate[layer], ffn_w_up[layer], ffn_w_down[layer])
    return rms_norm(x, final_norm_g)


_first_inputs = second_inputs


def second_inputs(seed=0):
    import zlib

    import numpy as np

    out = dict(_first_inputs(seed))
    spreads = {}
    factors = {'mix_norm_g': 2.711,
     'ffn_norm_g': 9.748,
     'final_norm_g': 8.72,
     'conv_dw_b': 16.926,
     'conv_ln_g': 49.16,
     'conv_ln_b': 61.76,
     'sgu_ln_g': 25.252,
     'sgu_ln_b': 25.594,
     'sgu_b': 51.982,
     'fnet_b_out': 32.2}
    for name, (base, spread) in spreads.items():
        noise = np.random.default_rng([zlib.crc32(name.encode()), seed]).standard_normal(out[name].shape)
        drawn = base * np.exp(spread * noise) if base else spread * noise
        out[name] = __import__('jax').numpy.asarray(drawn.astype(out[name].dtype))
    for name, factor in factors.items():
        out[name] = (out[name] * factor).astype(out[name].dtype)
    return out


_narrow_inputs = second_inputs


def second_inputs(seed=0):

    out = dict(_narrow_inputs(seed))
    wider = {'final_norm_g': 3.32,
     'conv_ln_g': 7.85,
     'conv_ln_b': 6.52,
     'sgu_ln_g': 5.7,
     'sgu_ln_b': 5.74,
     'sgu_b': 5.8,
     'fnet_w_out': 3.13,
     'fnet_b_out': 8.81}
    for name, times in wider.items():
        mean = out[name].mean()
        out[name] = (mean + times * (out[name] - mean)).astype(out[name].dtype)
    return out


def setup_inputs(seed=0):
    out = dict(first_inputs(seed))
    for name, value in second_inputs(seed + 1).items():
        if name != "x":
            out[name + "_2"] = value
    return out


def reference(
    x, c, ctx, c_ctx, w_mod, b_mod, norm_mix_pre, norm_mix_post, norm_mlp_pre, norm_mlp_post,
    w_mlp_in, w_mlp_out, s5_a_re, s5_a_im, s5_log_dt, s5_b_re, s5_b_im, s5_c_re, s5_c_im, s5_d,
    s5_w_glu, hg_w_in, hg_lb_raw, hg_o_norm, hg_w_out, mix_norm_g_2, ffn_norm_g_2,
    final_norm_g_2, ab_w_in_2, conv_dw_w_2, conv_dw_b_2, conv_ln_g_2, conv_ln_b_2, sgu_ln_g_2,
    sgu_ln_b_2, sgu_w_2, sgu_b_2, ab_w_out_2, fnet_w_out_2, fnet_b_out_2, ffn_w_gate_2,
    ffn_w_up_2, ffn_w_down_2,
):
    x = first_block(
        x, c, ctx, c_ctx, w_mod, b_mod, norm_mix_pre, norm_mix_post, norm_mlp_pre,
        norm_mlp_post, w_mlp_in, w_mlp_out, s5_a_re, s5_a_im, s5_log_dt, s5_b_re, s5_b_im,
        s5_c_re, s5_c_im, s5_d, s5_w_glu, hg_w_in, hg_lb_raw, hg_o_norm, hg_w_out,
    )
    return second_block(
        x, mix_norm_g_2, ffn_norm_g_2, final_norm_g_2, ab_w_in_2, conv_dw_w_2, conv_dw_b_2,
        conv_ln_g_2, conv_ln_b_2, sgu_ln_g_2, sgu_ln_b_2, sgu_w_2, sgu_b_2, ab_w_out_2,
        fnet_w_out_2, fnet_b_out_2, ffn_w_gate_2, ffn_w_up_2, ffn_w_down_2,
    )


_drawn_inputs = setup_inputs


def setup_inputs(seed=0):
    import zlib

    import numpy as np

    out = dict(_drawn_inputs(seed))
    spreads = {}
    factors = {}
    for name, (base, spread) in spreads.items():
        noise = np.random.default_rng([zlib.crc32(name.encode()), seed]).standard_normal(out[name].shape)
        drawn = base * np.exp(spread * noise) if base else spread * noise
        out[name] = __import__('jax').numpy.asarray(drawn.astype(out[name].dtype))
    for name, factor in factors.items():
        out[name] = (out[name] * factor).astype(out[name].dtype)
    return out
```

```python
from contextlib import ExitStack

import numpy as np

import concourse.bass as bass
from concourse import mybir

F32 = mybir.dt.float32
F32R = mybir.dt.float32r
I32 = mybir.dt.int32
ALU = mybir.AluOpType
ACT = mybir.ActivationFunctionType
AX = mybir.AxisListType

P = 128
D = 2048
KT = D // P
TOK = 256
L = 8
NCH = TOK // L
GRP, NST = 16, 64
GT = P // GRP
CB = GT
NCB = KT * CB
POW = L + 1
UK, UN = 4, 512
SLOTS = 4
NT = UN // P
EPS = 1e-6
LN_EPS = 1e-5
ds = bass.ds


def dft_tables():
    n = np.arange(TOK)
    ang = 2.0 * np.pi * ((n[:, None] * n[None, :]) % TOK) / TOK
    t = np.stack([np.cos(ang), np.sin(ang), -np.sin(ang)]) / np.sqrt(TOK)
    return np.ascontiguousarray(t.reshape(3, 2, P, TOK).transpose(2, 0, 1, 3).reshape(P, -1)).astype(np.float32)


def main_consts():
    c = np.zeros((P, 2 * P + 1), np.float32)
    c[:, :P] = np.eye(P)
    c[:, P:2 * P] = 1.0
    c[::32, 2 * P] = 1.0
    return c


def s5_consts():
    sel_g = np.zeros((P, 2, P // 2), np.float32)
    sel_c = np.zeros((P, 2, P // 2), np.float32)
    for g in range(P):
        sel_g[g, g % 2, g // 2] = 1.0
    for r in range(P):
        g, h = divmod(r, GRP)
        sel_c[r, g % 2, (g // 2) * GRP + h] = 1.0
    mask = np.ones((P, 2 * NCH), np.float32)
    mask[:, 0] = 0.0
    eye = np.tile(np.eye(GRP, dtype=np.float32), (GT, 1))
    eye_c = np.tile(np.eye(NCH, dtype=np.float32), (P // NCH, 1))
    return np.concatenate([sel_g.reshape(P, P), sel_c.reshape(P, P), mask, eye, eye_c], axis=1)


class Chain:

    def __init__(self, eng, sem, base=0):
        self.eng, self.sem, self.n, self.base = eng, sem, 0, base

    def __call__(self, ins):
        self.n += 1
        return ins.then_inc(self.sem, 1)

    def settle(self):
        self.eng.wait_ge(self.sem, self.base + self.n)


def two_layer_kernel(nc, a, out):
    ctx = ExitStack()
    with ctx:
        def sem(name):
            return ctx.enter_context(nc.semaphore(name))

        size_of = {F32: 4, F32R: 4, I32: 4}

        class Region:
            def __init__(self, start, end):
                self.at, self.end = start, end

            def __call__(self, name, shape, dt=F32):
                n = size_of[dt] * int(np.prod(shape[1:]))
                t = nc.alloc_sbuf_tensor_at(name, shape, dt, offset=self.at)
                self.at += (n + 31) // 32 * 32
                assert self.at <= self.end, (name, self.at - self.end)
                return t

        KB = 1024
        whole = Region((nc.sbuf_base + 63) // 64 * 64, nc.sbuf_usable_end)
        raw = whole("raw", [P, SLOTS, UK, UN])
        xin_at = whole.at
        xin = whole("xin", [P, KT, 2 * TOK], F32R)
        consts = whole("consts", [P, 2 * P + 1])
        ident, ones, quad = consts[:, 0:P], consts[:, P:2 * P], consts[:, 2 * P:2 * P + 1]
        par = whole("par", [P, 4 * P])
        ada = whole("ada", [P, 4 * KT])
        rstd_x = whole("rstd_x", [64, L])
        work_at = whole.at

        cols, at = {}, 0
        for name, n in [("b_mod", 64), ("mix_post", 16), ("mlp_pre", 16), ("mlp_post", 16), ("s5_d", 16),
                        ("mix_g", 32), ("ffn_g", 32), ("final_g", 16), ("fnet_b", 16), ("dw_b", 8),
                        ("cln_g", 8), ("cln_b", 8), ("sln_g", 8), ("sln_b", 8), ("dw_w", 248)]:
            cols[name] = at
            at += n
        assert at == 4 * P

        s5 = Region(work_at, whole.end)
        bb = s5("bb", [P, 2, NCB, GRP])
        lp = s5("lp", [P, 2, NCB, POW])
        ab = s5("ab", [P, 4, NCB, L])
        sb = s5("sb", [64, 2, D])
        xc = s5("xc", [64, L, P])
        xt = s5("xt", [64, GT, L, GRP])
        cond = s5("cond", [P, KT, 64])
        rows_at = s5.at
        bpow = s5("bpow", [P, 2, CB, P])
        cpow_at = s5.at
        cpow = [s5(f"cpow{i}", [P, 2, CB, POW * GRP]) for i in range(2)]
        craw_at = s5.at
        craw = s5("craw", [P, 2, 2, NST])
        ct = s5("ct", [P, 2, CB, GRP])
        ew_at = s5.at
        ew = s5("ew", [P, 2, CB, P])
        tw = s5("tw", [P, GT, P])
        rw_at = s5.at
        rw = s5("rw", [P, 15 * GRP])
        u_at = s5.at
        u = s5("u", [P, GT, 2 * NCH])
        bd = s5("bd", [P, CB, 2, 2, GRP])
        pt = s5("pt", [P, 2, CB, 2 * NCH])
        r8 = s5("r8", [P, CB, 2 * NCH])
        mz = s5("mz", [P, 2, CB, 2 * NCH])
        turned = s5("turned", [P, 2, CB, NCH])
        st = s5("st", [P, 2, CB, NCH])
        ptmp = s5("ptmp", [P, CB, POW * GRP])
        zt = s5("zt", [P, L, P])
        zt_end = s5.at
        s5c = s5("s5c", [P, 368])
        adarow = s5("adarow", [P, UN])
        r8all = s5("r8all", [P, NCB])
        sel_g, sel_c = s5c[:, 0:P], s5c[:, P:2 * P]
        mask, eye, eye_c = s5c[:, 256:320], s5c[:, 320:336], s5c[:, 336:368]
        braw = Region(cpow_at, craw_at)("braw", [P, 2, 2, NST * GRP])
        prow = Region(rows_at, cpow_at)
        prows = prow("prows", [P, 4, P])
        arow = prow("arow", [P, 3, P])
        ldt = prow("ldt", [P, 2])
        crow = prow("crow", [2 * KT, P])
        ss_sb = prow("ss_sb", [P, 4])
        tmps = Region(ew_at, rw_at)
        tv = [tmps(f"tv{i}", [P, NCB]) for i in range(24)]
        btmp = Region(u_at, zt_end)("btmp", [P, 2, NCB, GRP])
        lpr = Region(u_at, zt_end)
        lpa = lpr("lpa", [P, 2, NCB, POW])
        lpt = lpr("lpt", [P, 2, NCB, L // 2])
        xrow = Region(xin_at, xin_at + 32 * KB)
        bmod_row = xrow("bmod_row", [64, 2 * D])
        gain_row = xrow("gain_row", [64, D])
        xstat = xrow("xstat", [P, D])

        gm = Region(work_at, whole.end)
        w_hi = gm("w_hi", [P, SLOTS, UK * UN], F32R)
        w_lo = gm("w_lo", [P, SLOTS, UK * UN], F32R)
        hid_at = gm.at
        hid = gm("hid", [P, KT, 2 * TOK], F32R)
        y_at = gm.at
        y = gm("y", [P, KT, TOK])
        xr = gm("xr", [P, KT, TOK])
        tmp = gm("tmp", [P, 2, NT, TOK])
        rs = gm("rs", [P, 2, TOK])
        conv_tmp = gm("conv_tmp", [P, 2, TOK])
        coef = gm("coef", [P, 3 * KT])
        x_rows = Region(hid_at, y_at)("x_rows", [P, 2, D])
        z = Region(hid_at, y_at)("z", [P, 2 * KT, TOK])
        hf = Region(hid_at, y_at)("hf", [P, KT, TOK])
        out_rows = Region(hid_at + 16 * KB, y_at)("out_rows", [P, 4, D // 2])
        sq_x = Region(xin_at, xin_at + 32 * KB)("sq_x", [P, KT, TOK])
        QZ = 8 * KB
        wsr = Region(hid_at + QZ, hid_at + QZ + 4 * KB)("wsr", [P, 8, P])
        wst = Region(hid_at + QZ + 4 * KB, hid_at + 2 * QZ)("wst", [P, 8, P])
        vt = Region(hid_at + 3 * QZ, y_at)("vt", [P, 2, 8, P])
        W_CONV, PAD = 31, 15
        CONV_POOL = 2
        pad_w = TOK + 2 * PAD
        conv_in = Region(y_at, y_at + 16 * KB)("conv_in", [P, 8, pad_w])
        conv_sq = Region(y_at, y_at + QZ)("conv_sq", [P, 8, TOK])
        sgub = Region(y_at + 15 * KB, y_at + 16 * KB)("sgub", [8, P])
        dft = Region(y_at, y_at + 16 * KB)("dft", [P, 3, 2, TOK])

        acc = ctx.enter_context(nc.psum_tensor("acc", [P, 8, 512], F32))
        ps = [acc[:, i, :] for i in range(8)]

        r_dram = nc.dram_tensor("r_scratch", [GT, GRP, 15 * GRP], F32, kind="Internal").ap()
        ss_dram = nc.dram_tensor("ss_scratch", [2 * TOK], F32, kind="Internal").ap()
        x2, ctx2 = a["x"][0], a["ctx"][0]
        xch = [ctx2.rearrange("(c j) d -> c j d", j=L), x2.rearrange("(c j) d -> c j d", j=L)]
        w_mod = a["w_mod"][0].rearrange("(k p) n -> p k n", p=P)
        c_view = [a["s5_c_re"][0].rearrange("d (k g) h p -> k (g h) d p", g=GT),
                  a["s5_c_im"][0].rearrange("d (k g) h p -> k (g h) d p", g=GT)]
        b_view = [a["s5_b_re"][0].rearrange("d g p h -> g d (p h)"), a["s5_b_im"][0].rearrange("d g p h -> g d (p h)")]

        def rows(v):
            return v.rearrange("(r p) -> r p", p=P)

        par_src = [rows(a["b_mod"][0][2 * D:6 * D]), rows(a["norm_mix_post"][0]), rows(a["norm_mlp_pre"][0]),
                   rows(a["norm_mlp_post"][0]), rows(a["s5_d"][0]),
                   a["mix_norm_g_2"].rearrange("l (r p) -> (l r) p", p=P),
                   a["ffn_norm_g_2"].rearrange("l (r p) -> (l r) p", p=P),
                   rows(a["final_norm_g_2"]), rows(a["fnet_b_out_2"][0]), rows(a["conv_dw_b_2"][0]),
                   rows(a["conv_ln_g_2"][0]), rows(a["conv_ln_b_2"][0]), rows(a["sgu_ln_g_2"][0]),
                   rows(a["sgu_ln_b_2"][0]), a["conv_dw_w_2"][0].rearrange("w (r p) -> (w r) p", p=P)]
        par_dma, at = [], 0
        for v in par_src:
            n, done = v.shape[0], 0
            while done < n:
                k = min(n - done, P - at % P)
                par_dma.append((at // P, at % P, k, v[done:done + k, :]))
                at += k
                done += k

        const_in = sem("const_in")
        s5p_in = sem("s5p_in")
        rows_in = sem("rows_in")
        xstat_in = sem("xstat_in")
        xstat_sq = sem("xstat_sq")
        ss_out = sem("ss_out")
        ss_in = sem("ss_in")
        ss_ready = sem("ss_ready")
        rstd_ready = sem("rstd_ready")
        rstd_root = sem("rstd_root")
        raw_ready = [sem(f"raw_ready{s}") for s in range(SLOTS)]
        ada_unit = sem("ada_unit")
        cond_silu, cond_tr, cond_ready = sem("cond_silu"), sem("cond_tr"), sem("cond_ready")
        par_tr, par_sb = sem("par_tr"), sem("par_sb")
        ldt_wide = sem("ldt_wide")
        a_tr = sem("a_tr")
        b_sel, b_sb = sem("b_sel"), sem("b_sb")
        angle_ready, sin_ready = sem("angle_ready"), sem("sin_ready")
        tables_ready = sem("tables_ready")
        prep = sem("prep")
        ada1_sb = sem("ada1_sb")
        pool_prep = sem("pool_prep")
        mod_ready = sem("mod_ready")
        x_tile, c_tile = sem("x_tile"), sem("c_tile")
        xt_scaled, xt_done = sem("xt_scaled"), sem("xt_done")
        u_tr, u_sb = sem("u_tr"), sem("u_sb")
        v_done, s_done, y_done = sem("v_done"), sem("s_done"), sem("y_done")
        y_gelu, zt_zero, z_tr, z_hi, z_lo = (sem(n) for n in ("y_gelu", "zt_zero", "z_tr", "z_hi", "z_lo"))
        c_sel, c_sb, cpow_done = sem("c_sel"), sem("c_sb"), sem("cpow_done")
        k_done, r_sb, r_out, t_in = sem("k_done"), sem("r_sb"), sem("r_out"), sem("t_in")
        bpow_done, e_tr, e_sb, bd_sb = sem("bpow_done"), sem("e_tr"), sem("e_sb"), sem("bd_sb")
        ada_sb, ada_col, ada_done = sem("ada_sb"), sem("ada_col"), sem("ada_done")
        dve_step, pool_step = sem("dve_step"), sem("pool_step")

        ADA_UNITS = 32 + 4 * KT
        FF = a["ffn_w_gate_2"].shape[2]
        FULL = FF // (KT * P)
        REST = FF % (KT * P) // UN
        MLP_PARTS = a["w_mlp_in"].shape[2] // (KT * P)

        def wv(v):
            return v.rearrange("(k p) n -> p k n", p=P)

        w_glu, w_in, w_out = wv(a["s5_w_glu"][0]), wv(a["w_mlp_in"][0]), wv(a["w_mlp_out"][0])
        w_ab_in, w_ab_out, w_fnet = wv(a["ab_w_in_2"][0]), wv(a["ab_w_out_2"][0]), wv(a["fnet_w_out_2"][0])
        w_gate = [wv(a["ffn_w_gate_2"][l]) for l in range(2)]
        w_up = [wv(a["ffn_w_up_2"][l]) for l in range(2)]
        w_down = [wv(a["ffn_w_down_2"][l]) for l in range(2)]

        GLU, MLP = (0, 0), (32, 8)
        AB_IN = (MLP[0] + 32 * MLP_PARTS, MLP[1] + 8 * MLP_PARTS)
        AB_OUT = (AB_IN[0] + 32, AB_IN[1] + 8)
        FFN0 = (AB_OUT[0] + 16, AB_OUT[1] + 4)
        FFN_UNITS, FFN_BLOCKS = 48 * FULL + 8 * REST + 4 * REST, 12 * FULL + 2 * REST + 4
        FNET = (FFN0[0] + FFN_UNITS, FFN0[1] + FFN_BLOCKS)
        FFN1 = (FNET[0] + 16, FNET[1] + 4)
        UNITS, BLOCKS = FFN1[0] + FFN_UNITS, FFN1[1] + FFN_BLOCKS
        HID0, HID1 = 4 * MLP_PARTS, 4 * MLP_PARTS + 4 * FULL + REST
        Y_MLP, Y_FFN0 = 1 + 4, 1 + 4 + 4 * MLP_PARTS
        Y_FFN1 = Y_FFN0 + 4 * (FULL + 1)
        CH = 4
        NCK = KT // CH
        X_SEAM = {0: 0, 1: NCK, 2: 3 * NCK, 4: 4 * NCK}
        X_MIX = 2 * NCK

        (hi_ready, lo_ready, pe_unit, folded, gate_act, h_ready, hid_hi, hid_ready, y_added, y_zero, x_rows_in,
         x_rows_tr, coef_ready, xin_hi, xin_ready, y_sq, y_sum, y_ms, y_root, y_rs, y_normed, x_new, x_sq, x_sum,
         x_ms, x_root, x_rs, xn_ready, xn_shifted, gate_sig, pad_zero, conv_in_ready, conv_in2_ready, conv_dve,
         conv_pool, conv_mul, conv_mean, conv_centred, conv_sqd, conv_var, conv_ms, conv_root, conv_rs, conv_normed,
         conv_out, u_gelu, v_gelu, v_mean, v_mu, v_centred, v_sqd, v_var, v_ms, v_root, v_rs, v_scaled, v_out, v_tr,
         v_sb, sgu_in, ws_tr, ws_sb, mixed, gated, dft_in, f1_done, f1_sb, f2_done, f_hi, f_lo, final_tr, final_sb,
         out_done) = (sem(n) for n in """
            hi_ready lo_ready pe_unit folded gate_act h_ready hid_hi hid_ready y_added y_zero x_rows_in x_rows_tr
            coef_ready xin_hi xin_ready y_sq y_sum y_ms y_root y_rs y_normed x_new x_sq x_sum x_ms x_root x_rs
            xn_ready xn_shifted gate_sig pad_zero conv_in_ready conv_in2_ready conv_dve conv_pool conv_mul conv_mean
            conv_centred conv_sqd conv_var conv_ms conv_root conv_rs conv_normed conv_out u_gelu v_gelu v_mean v_mu
            v_centred v_sqd v_var v_ms v_root v_rs v_scaled v_out v_tr v_sb sgu_in ws_tr ws_sb mixed gated dft_in
            f1_done f1_sb f2_done f_hi f_lo final_tr final_sb out_done""".split())

        class Seam:
            def __init__(self, n, block, post, gain, shift, sq, to_xin):
                self.n, self.block, self.post, self.gain, self.shift = n, block, post, gain, shift
                self.sq, self.to_xin = sq, to_xin
                self.x0 = X_SEAM.get(n)

        def pcol(name, off=0):
            return lambda k: par[:, cols[name] + off + k:cols[name] + off + k + 1]

        SEAMS = [
            Seam(0, MLP[1], lambda k: coef[:, k:k + 1], lambda k: coef[:, KT + k:KT + k + 1],
                 lambda k: ada[:, KT + k:KT + k + 1], hf, True),
            Seam(1, AB_IN[1], lambda k: coef[:, 2 * KT + k:2 * KT + k + 1], pcol("mix_g"), None, sq_x, True),
            Seam(2, FFN0[1], None, pcol("ffn_g"), None, hf, True),
            Seam(3, FNET[1], None, pcol("mix_g", KT), None, sq_x, False),
            Seam(4, FFN1[1], None, pcol("ffn_g", KT), None, hf, True),
            Seam(5, BLOCKS, None, pcol("final_g"), None, sq_x, False),
        ]

        def GEMM_SP(sp):
            def unit(u, slot, src, k, col, early=None):
                if early is not None and early < SLOTS:
                    sp.wait_ge(ada_unit, ADA_UNITS - SLOTS + early + 1)
                else:
                    sp.wait_ge(lo_ready, u - (SLOTS - 1))
                sp.dma_start(raw[:, slot, :, :], src[:, ds(k * UK, UK), ds(col, UN)]).then_inc(raw_ready[slot], 16)

            def block_(u, src, col, k0=0):
                for k in range(4):
                    unit(u + k, k, src, k0 + k, col)

            for k in range(4):
                unit(k, k, w_glu, k, 0, early=k)
            sp.wait_ge(z_lo, KT)
            sp.wait_ge(ada_done, KT)
            for t in range(2):
                sp.dma_start(x_rows[:, t, :], x2[t * P:(t + 1) * P, :]).then_inc(x_rows_in, 16)
            block_(4, w_glu, D)

            def glu(i):
                block_(8 * i, w_glu, i * UN)
                block_(8 * i + 4, w_glu, i * UN + D)
            with sp.Fori(1, 4) as i:
                glu(i)
            with sp.Fori(0, MLP_PARTS) as q:
                with sp.Fori(0, 4) as i:
                    block_(32 * q + (4 * i + MLP[0]), w_in, q * (4 * UN) + i * UN)
                with sp.Fori(0, 4) as i:
                    block_(32 * q + (4 * i + (MLP[0] + 16)), w_out, i * UN, q * 4)
            with sp.Fori(0, 2) as i:
                block_(8 * i + AB_IN[0], w_ab_in, i * UN)
                block_(8 * i + (AB_IN[0] + 4), w_ab_in, i * UN + D // 2)
            with sp.Fori(0, 4) as i:
                block_(4 * i + (AB_IN[0] + 16), w_ab_in, i * UN + D)
            sp.wait_ge(conv_in_ready, 1)
            sp.wait_ge(conv_in2_ready, 1)
            sp.dma_start(sgub[:, :], a["sgu_b_2"][0]).then_inc(sgu_in, 16)
            sp.dma_start(wsr[:, :, :], a["sgu_w_2"][0].rearrange("h p q -> p h q")).then_inc(sgu_in, 16)
            with sp.Fori(0, 4) as i:
                block_(4 * i + AB_OUT[0], w_ab_out, i * UN)

            def ffn(l, base):
                with sp.Fori(0, FULL) as q:
                    with sp.Fori(0, 4) as i:
                        block_(48 * q + (8 * i + base), w_gate[l], q * (4 * UN) + i * UN)
                        block_(48 * q + (8 * i + (base + 4)), w_up[l], q * (4 * UN) + i * UN)
                    with sp.Fori(0, 4) as i:
                        block_(48 * q + (4 * i + (base + 32)), w_down[l], i * UN, q * 4)
                b2 = base + 48 * FULL
                with sp.Fori(0, REST) as i:
                    block_(8 * i + b2, w_gate[l], i * UN + FULL * 4 * UN)
                    block_(8 * i + (b2 + 4), w_up[l], i * UN + FULL * 4 * UN)
                b3 = b2 + 8 * REST
                for v in range(4 * REST):
                    unit(b3 + v, v % SLOTS, w_down[l], 4 * FULL + v % REST, v // REST * UN)

            ffn(0, FFN0[0])
            block_(FNET[0], w_fnet, 0)
            sp.wait_ge(x_new, 4 * NCK)
            sp.dma_start(dft[:, :, :, :].rearrange("p a b c -> p (a b c)"), a["c_dft"]).then_inc(dft_in, 16)
            with sp.Fori(1, 4) as i:
                block_(4 * i + FNET[0], w_fnet, i * UN)
            ffn(1, FFN1[0])
            for t in range(4):
                dh, th = divmod(t, 2)
                sp.wait_ge(final_sb, t + 1)
                sp.dma_start(out[0, th * P:(th + 1) * P, dh * (D // 2):(dh + 1) * (D // 2)],
                             out_rows[:, t, :]).then_inc(out_done, 16)
            sp.wait_ge(out_done, 64)

        def GEMM_PE(pe):
            def block_(u, blk, half, operand, ready=None, units=4, slot0=0):
                pe.wait_ge(folded, blk + 1)
                for k in range(units):
                    slot = (slot0 + k) % SLOTS
                    if ready is not None:
                        ready(k)
                    pe.wait_ge(lo_ready, u + (k + 1))
                    for q in range(UK):
                        for n in range(NT):
                            w = slice(q * UN + n * P, q * UN + (n + 1) * P)
                            bank, kt = ps[4 * half + n], UK * k + q
                            pe.matmul(bank, w_hi[:, slot, w], operand[:, kt, :], start=(kt == 0), stop=False)
                            ins = pe.matmul(bank[:, 0:TOK], w_lo[:, slot, w], operand[:, kt, 0:TOK],
                                            start=False, stop=(kt == UK * units - 1))
                    ins.then_inc(pe_unit, 1)

            def xin_from(base):
                return lambda k: pe.wait_ge(xin_ready, base + k + 1)

            def hid_from(part):
                return lambda k: pe.wait_ge(hid_ready, part + (k + 2))

            def seam(s):
                pe.wait_ge(folded, s.block + 1)
                if s.post:
                    for c in range(NCK):
                        pe.wait_ge(y_sq, NCK * s.n + c + 1)
                        for k in range(CH * c, CH * (c + 1)):
                            ins = pe.matmul(ps[0][:, 0:TOK], ones, s.sq[:, k, :], start=(k == 0), stop=(k == KT - 1))
                    ins.then_inc(y_sum, 1)
                for c in range(NCK):
                    pe.wait_ge(x_sq, NCK * s.n + c + 1)
                    for k in range(CH * c, CH * (c + 1)):
                        ins = pe.matmul(ps[1][:, 0:TOK], ones, s.sq[:, k, :], start=(k == 0), stop=(k == KT - 1))
                ins.then_inc(x_sum, 1)

            def mixer():
                pe.wait_ge(folded, AB_OUT[1] + 2)
                pe.wait_ge(sgu_in, 32)
                for h in range(8):
                    ins = pe.transpose(ps[5 + h // 4][:, h % 4 * P:(h % 4 + 1) * P], wsr[:, h, :], ident)
                ins.then_inc(ws_tr, 1)
                pe.wait_ge(conv_dve, (8 - CONV_POOL) * W_CONV)
                pe.wait_ge(conv_pool, CONV_POOL * W_CONV)
                for k in range(8):
                    ins = pe.matmul(ps[k // 2][:, k % 2 * TOK:(k % 2 + 1) * TOK], ones, z[:, k, :], start=True, stop=True)
                ins.then_inc(conv_mean, 1)
                pe.wait_ge(v_gelu, 1)
                for k in range(8):
                    ins = pe.matmul(ps[4][:, 0:TOK], ones, z[:, 24 + k, :], start=(k == 0), stop=(k == 7))
                ins.then_inc(v_mean, 1)
                pe.wait_ge(conv_sqd, 1)
                for k in range(8):
                    ins = pe.matmul(ps[k // 2][:, k % 2 * TOK:(k % 2 + 1) * TOK], ones, conv_sq[:, k, :], start=True, stop=True)
                ins.then_inc(conv_var, 1)
                pe.wait_ge(v_sqd, 1)
                for k in range(8):
                    ins = pe.matmul(ps[7][:, 0:TOK], ones, tmp[:, k // 4, k % 4, :], start=(k == 0), stop=(k == 7))
                ins.then_inc(v_var, 1)
                pe.wait_ge(v_out, 1)
                pe.wait_ge(conv_ms, 1)
                for n in range(2):
                    for h in range(8):
                        ins = pe.transpose(ps[2 * n + h // 4][:, h % 4 * P:(h % 4 + 1) * P], z[:, 24 + h, n * P:(n + 1) * P], ident)
                ins.then_inc(v_tr, 1)
                pe.wait_ge(ws_sb, 1)

                def mixed_to(h, n):
                    return ps[4 + h // 2][:, h % 2 * TOK + n * P:h % 2 * TOK + (n + 1) * P]

                pe.wait_ge(v_sb, 1)
                for h in range(8):
                    for n in range(2):
                        pe.matmul(mixed_to(h, n), ident[0:8, h:h + 1].broadcast_to([8, P]), sgub[:, :], start=True, stop=False)
                        ins = pe.matmul(mixed_to(h, n), vt[:, n, h, :], wst[:, h, :], start=False, stop=True)
                    if h % 4 == 3:
                        ins.then_inc(mixed, 1)

            def fourier():
                pe.wait_ge(folded, FNET[1] + 2)
                pe.wait_ge(dft_in, 16)

                def channels(g):
                    pe.wait_ge(xn_ready, NCK * 3 + g // 2 + 1)
                    if g >= 2:
                        pe.wait_ge(f1_sb, g - 1)
                    for t in range(2):
                        for dt in range(2):
                            ins = pe.matmul(ps[2 * (g % 2) + t], hf[:, 2 * g + dt, t * P:(t + 1) * P], dft[:, 0:2, dt, :],
                                            start=(dt == 0), stop=(dt == 1))
                    ins.then_inc(f1_done, 1)

                def tokens(g):
                    pe.wait_ge(f1_sb, g + 1)
                    if g >= 2:
                        pe.wait_ge(f_lo, g - 1)
                    for k in range(2):
                        o = ps[4 + g % 2][:, k * TOK:(k + 1) * TOK]
                        for t in range(2):
                            for cs in range(2):
                                ins = pe.matmul(o, tmp[:, g % 2, 2 * t + cs, k * P:(k + 1) * P], dft[:, 2 * cs, t, :],
                                                start=(t + cs == 0), stop=(t + cs == 2))
                    ins.then_inc(f2_done, 1)

                channels(0)
                for g in range(1, 8):
                    channels(g)
                    tokens(g - 1)
                tokens(7)

            def ffn(base, x0, hid0):
                u0, b0 = base

                def gate_up(u, blk):
                    block_(u, blk, 0, xin, xin_from(x0))
                    block_(u + 4, blk + 1, 1, xin)

                with pe.Fori(0, FULL) as q:
                    with pe.Fori(0, 4) as i:
                        gate_up(48 * q + (8 * i + u0), 12 * q + (2 * i + b0))
                    with pe.Fori(0, 2) as i:
                        for j in range(2):
                            block_(48 * q + (8 * i + (u0 + 32 + 4 * j)), 12 * q + (2 * i + (b0 + 8 + j)), j, hid,
                                   hid_from(4 * q + hid0))
                u1, b1 = u0 + 48 * FULL, b0 + 12 * FULL
                with pe.Fori(0, REST) as i:
                    gate_up(8 * i + u1, 2 * i + b1)
                u2, b2 = u1 + 8 * REST, b1 + 2 * REST
                for n in range(4):
                    block_(u2 + REST * n, b2 + n, n % 2, hid, hid_from(hid0 + 4 * FULL), REST, REST * n % SLOTS)

            pe.wait_ge(x_rows_in, 32)
            pe.wait_ge(z_lo, KT)
            pe.wait_ge(ada_done, KT)
            for k in range(KT):
                for t in range(2):
                    ins = pe.transpose(ps[k // 2][:, k % 2 * TOK + t * P:k % 2 * TOK + (t + 1) * P], x_rows[:, t, k * P:(k + 1) * P], ident)
                if k % 8 == 7:
                    ins.then_inc(x_rows_tr, 1)
            with pe.Fori(0, 4) as i:
                for j in range(2):
                    block_(8 * i + 4 * j, 2 * i + j, j, xin)
            seam(SEAMS[0])
            with pe.Fori(0, MLP_PARTS) as q:
                with pe.Fori(0, 2) as i:
                    for j in range(2):
                        block_(32 * q + (8 * i + (MLP[0] + 4 * j)), 8 * q + (2 * i + (MLP[1] + j)), j, xin, xin_from(X_SEAM[0]))
                with pe.Fori(0, 2) as i:
                    for j in range(2):
                        block_(32 * q + (8 * i + (MLP[0] + 16 + 4 * j)), 8 * q + (2 * i + (MLP[1] + 4 + j)), j, hid, hid_from(4 * q))
            seam(SEAMS[1])
            with pe.Fori(0, 4) as i:
                for j in range(2):
                    block_(8 * i + (AB_IN[0] + 4 * j), 2 * i + (AB_IN[1] + j), j, xin, xin_from(X_SEAM[1]))
            mixer()
            with pe.Fori(0, 2) as i:
                for j in range(2):
                    block_(8 * i + (AB_OUT[0] + 4 * j), 2 * i + (AB_OUT[1] + j), j, xin, xin_from(X_MIX))
            seam(SEAMS[2])
            ffn(FFN0, X_SEAM[2], HID0)
            seam(SEAMS[3])
            fourier()
            with pe.Fori(0, 2) as i:
                for j in range(2):
                    block_(8 * i + (FNET[0] + 4 * j), 2 * i + (FNET[1] + j), j, xin,
                           lambda k: pe.wait_ge(f_lo, 2 * (k + 1)))
            seam(SEAMS[4])
            ffn(FFN1, X_SEAM[4], HID1)
            seam(SEAMS[5])
            for t in range(4):
                dh, th = divmod(t, 2)
                for k in range(8):
                    pe.wait_ge(xn_ready, NCK * 5 + 2 * dh + k // 4 + 1)
                    ins = pe.transpose(ps[2 * t + k // 4][:, k % 4 * P:(k % 4 + 1) * P], hf[:, 8 * dh + k, th * P:(th + 1) * P], ident)
                ins.then_inc(final_tr, 1)

        def GEMM_ACT(act):
            def split_unit(u, slot, dma, early=False):
                act.wait_ge(raw_ready[slot], dma)
                if not early:
                    act.wait_ge(pe_unit, u - (SLOTS - 1))
                act.activation(w_hi[:, slot, :], raw[:, slot, :, :].rearrange("p k n -> p (k n)"), ACT.Copy).then_inc(hi_ready, 1)

            ADA_DMA = ADA_UNITS // SLOTS

            def split(grp, early=False, slots=range(SLOTS)):
                for slot in slots:
                    split_unit(4 * grp + slot, slot, 16 * grp + 16 * (ADA_DMA + 1), early)

            def seam(s):
                if s.post:
                    for c in range(NCK):
                        act.wait_ge(y_added, (Y_MLP, Y_FFN0)[s.n] - NCK + c + 1)
                        act.activation(s.sq[:, CH * c:CH * (c + 1), :], y[:, CH * c:CH * (c + 1), :], ACT.Square).then_inc(y_sq, 1)
                    act.wait_ge(y_ms, s.n + 1)
                    act.activation(rs[:, 0, :], rs[:, 0, :], ACT.Sqrt).then_inc(y_root, 1)
                for c in range(NCK):
                    act.wait_ge(x_new, NCK * s.n + c + 1)
                    act.activation(s.sq[:, CH * c:CH * (c + 1), :], xr[:, CH * c:CH * (c + 1), :], ACT.Square).then_inc(x_sq, 1)
                act.wait_ge(x_ms, s.n + 1)
                act.activation(rs[:, 1, :], rs[:, 1, :], ACT.Sqrt).then_inc(x_root, 1)
                if s.to_xin:
                    for c in range(NCK):
                        act.wait_ge(xn_ready, NCK * s.n + c + 1)
                        if s.shift:
                            for k in range(CH * c, CH * (c + 1)):
                                ins = act.activation(hf[:, k, :], hf[:, k, :], ACT.Identity, bias=s.shift(k))
                            ins.then_inc(xn_shifted, 1)
                            act.wait_ge(xn_shifted, c + 1)
                        act.activation(xin[:, CH * c:CH * (c + 1), 0:TOK], hf[:, CH * c:CH * (c + 1), :], ACT.Copy).then_inc(xin_hi, 1)

            def hidden(n, chunk, half):
                act.wait_ge(h_ready, n + 1)
                act.activation(hid[:, ds(CH * chunk, CH) if not isinstance(chunk, int) else slice(CH * chunk, CH * (chunk + 1)), 0:TOK],
                               tmp[:, half], ACT.Copy).then_inc(hid_hi, 1)

            def ffn(base, g0, hid0, gate0):
                b0 = base[1]

                def gate_up(grp, blk, n, chunk):
                    split(grp + 1)
                    act.wait_ge(folded, blk + 3)
                    act.activation(tmp[:, 0], tmp[:, 0], ACT.Silu).then_inc(gate_act, 1)
                    split(grp + 2)
                    hidden(n, chunk, 1)

                with act.Fori(0, FULL) as q:
                    with act.Fori(0, 4) as i:
                        gate_up(12 * q + (2 * i + g0), 12 * q + (2 * i + b0), 4 * q + (i + hid0), i)
                    with act.Fori(0, 4) as i:
                        split(12 * q + (i + (g0 + 9)))
                g1, b1, h1 = g0 + 12 * FULL, b0 + 12 * FULL, hid0 + 4 * FULL
                with act.Fori(0, REST) as i:
                    gate_up(2 * i + g1, 2 * i + b1, i + h1, i)
                g2 = g1 + 2 * REST
                for g in range(1, REST):
                    split(g2 + g)

            act.wait_ge(z_lo, KT)
            act.wait_ge(ada_done, KT)
            split(0, early=True)
            with act.Fori(0, 4) as i:
                split(2 * i + 1)
                split(2 * i + 2)
                act.wait_ge(folded, 2 * i + 4)
                act.activation(tmp[:, 1], tmp[:, 1], ACT.Sigmoid).then_inc(gate_act, 1)
            seam(SEAMS[0])
            G = MLP[0] // 4
            with act.Fori(0, MLP_PARTS) as q:
                with act.Fori(0, 2) as i:
                    for j in range(2):
                        split(8 * q + (2 * i + (G + 1 + j)))
                        hidden(4 * q + (2 * i + j), 2 * i + j, j)
                with act.Fori(0, 4) as i:
                    split(8 * q + (i + (G + 5)))
            seam(SEAMS[1])
            G = AB_IN[0] // 4
            for half in range(2):
                split(G + 1 + 2 * half)
                split(G + 2 + 2 * half)
                act.wait_ge(folded, AB_IN[1] + 2 * half + 2 + 2)
                gate = z[:, 8 + 4 * half:12 + 4 * half, :]
                act.activation(gate, gate, ACT.Sigmoid).then_inc(gate_sig, 1)
            with act.Fori(0, 2) as i:
                split(i + (G + 5))
            act.wait_ge(folded, AB_IN[1] + 6 + 2)
            act.activation(z[:, 16:24, :], z[:, 16:24, :], ACT.Gelu).then_inc(u_gelu, 1)
            with act.Fori(0, 2) as i:
                split(i + (G + 7))
            act.wait_ge(folded, AB_IN[1] + 8 + 2)
            act.activation(z[:, 24:32, :], z[:, 24:32, :], ACT.Gelu).then_inc(v_gelu, 1)
            act.wait_ge(ws_tr, 1)
            act.activation(wst[:, :, :], acc[:, 5:7, :].rearrange("p b (h q) -> p (b h) q", q=P), ACT.Copy).then_inc(ws_sb, 1)
            act.wait_ge(conv_centred, 1)
            act.activation(conv_sq[:, :, :], z[:, 0:8, :], ACT.Square).then_inc(conv_sqd, 1)
            act.wait_ge(v_centred, 1)
            act.activation(tmp[:, :, :, :].rearrange("p a b t -> p (a b) t"), z[:, 24:32, :], ACT.Square).then_inc(v_sqd, 1)
            act.wait_ge(v_ms, 1)
            act.activation(rs[:, 0, :], rs[:, 0, :], ACT.Sqrt).then_inc(v_root, 1)
            act.wait_ge(conv_ms, 1)
            act.activation(conv_sq[:, :, :], conv_sq[:, :, :], ACT.Sqrt).then_inc(conv_root, 1)
            act.wait_ge(v_tr, 1)
            act.activation(vt[:, :, :, :].rearrange("p n h c -> p (n h c)"), acc[:, 0:4, :].rearrange("p b n -> p (b n)"), ACT.Copy).then_inc(v_sb, 1)
            act.wait_ge(conv_normed, 1)
            for c in range(2):
                for k in range(CH * c, CH * (c + 1)):
                    ins = act.activation(z[:, k, :], z[:, k, :], ACT.Silu, bias=par[:, cols["cln_b"] + k:cols["cln_b"] + k + 1],
                                         scale=par[:, cols["cln_g"] + k:cols["cln_g"] + k + 1])
                ins.then_inc(conv_out, 1)
            for c in range(2):
                act.wait_ge(conv_out, c + 1)
                act.activation(xin[:, CH * c:CH * (c + 1), 0:TOK], z[:, CH * c:CH * (c + 1), :], ACT.Copy).then_inc(xin_hi, 1)
            for c in range(2):
                act.wait_ge(gated, c + 1)
                act.activation(xin[:, CH * (c + 2):CH * (c + 3), 0:TOK], z[:, 16 + CH * c:16 + CH * (c + 1), :], ACT.Copy).then_inc(xin_hi, 1)
            G = AB_OUT[0] // 4
            with act.Fori(0, 4) as i:
                split(i + (G + 1))
            seam(SEAMS[2])
            ffn(FFN0, FFN0[0] // 4, HID0, 4)
            split(FNET[0] // 4)
            seam(SEAMS[3])
            for g in range(8):
                act.wait_ge(f2_done, g + 1)
                act.activation(xin[:, 2 * g:2 * g + 2, 0:TOK], ps[4 + g % 2].rearrange("p (k t) -> p k t", k=2), ACT.Copy).then_inc(f_hi, 1)
            G = FNET[0] // 4
            with act.Fori(0, 4) as i:
                split(i + (G + 1))
            seam(SEAMS[4])
            ffn(FFN1, FFN1[0] // 4, HID1, 4 + HID1 - HID0)
            seam(SEAMS[5])
            for t in range(4):
                act.wait_ge(final_tr, t + 1)
                act.activation(out_rows[:, t, :], acc[:, 2 * t:2 * t + 2, :].rearrange("p b n -> p (b n)"), ACT.Copy).then_inc(final_sb, 1)

        def GEMM_DVE(dve):
            MUL, ADD, SUB = ALU.mult, ALU.add, ALU.subtract

            def split(grp, slots=range(SLOTS)):
                for slot in slots:
                    dve.wait_ge(hi_ready, 4 * grp + (slot + 1))
                    dve.tensor_tensor(w_lo[:, slot, :], raw[:, slot, :, :].rearrange("p k n -> p (k n)"),
                                      w_hi[:, slot, :].bitcast(F32), SUB).then_inc(lo_ready, 1)

            def fold(units_done, half, dst, done=None):
                dve.wait_ge(pe_unit, units_done)
                dve.tensor_reduce(dst, acc[:, 4 * half:4 * half + 4, :].rearrange("p a (t b) -> p a b t", t=2),
                                  AX.X, ADD).then_inc(folded, 1)

            def chunk(c):
                return slice(CH * c, CH * (c + 1)) if isinstance(c, int) else ds(CH * c, CH)

            def rest(dst, src, k, done):
                return dve.tensor_tensor(dst[:, k, TOK:2 * TOK], src, dst[:, k, 0:TOK].bitcast(F32), SUB).then_inc(done, 1)

            def rsqrt(n, src, part, ms, root, done, width, eps):
                dve.tensor_scalar(rs[:, part, :], src, 1.0 / width, eps, MUL, ADD).then_inc(ms, 1)
                dve.wait_ge(root, n)
                dve.reciprocal(rs[:, part, :], rs[:, part, :]).then_inc(done, 1)
                dve.wait_ge(done, n)

            def seam(s):
                n = s.n
                if s.post:
                    dve.wait_ge(y_sum, n + 1)
                    rsqrt(n + 1, ps[0][:, 0:TOK], 0, y_ms, y_root, y_rs, D, EPS)
                    for c in range(NCK):
                        for k in range(CH * c, CH * (c + 1)):
                            ins = dve.scalar_tensor_tensor(y[:, k, :], y[:, k, :], s.post(k), rs[:, 0, :], MUL, MUL)
                        ins.then_inc(y_normed, 1)
                        dve.wait_ge(y_normed, NCK * n + c + 1)
                        dve.tensor_tensor(xr[:, chunk(c), :], xr[:, chunk(c), :], y[:, chunk(c), :], ADD).then_inc(x_new, 1)
                dve.wait_ge(x_sum, n + 1)
                rsqrt(n + 1, ps[1][:, 0:TOK], 1, x_ms, x_root, x_rs, D, EPS)
                for c in range(NCK + 1):
                    if c < NCK:
                        for k in range(CH * c, CH * (c + 1)):
                            ins = dve.scalar_tensor_tensor(hf[:, k, :], xr[:, k, :], s.gain(k), rs[:, 1, :], MUL, MUL)
                        ins.then_inc(xn_ready, 1)
                    if c and s.to_xin:
                        dve.wait_ge(xin_hi, s.x0 + c)
                        rest(xin, hf[:, chunk(c - 1), :], chunk(c - 1), xin_ready)

            def hidden(n, c, half):
                dve.wait_ge(hid_hi, n + 1)
                rest(hid, tmp[:, half], chunk(c), hid_ready)

            def add_to_y(units, blk, half, c, n, hidden_before):
                dve.wait_ge(hid_ready, hidden_before)
                dve.wait_ge(y_added, n)
                fold(units, half, tmp[:, half])
                dve.wait_ge(folded, blk + 3)
                dve.tensor_tensor(y[:, chunk(c), :], y[:, chunk(c), :], tmp[:, half], ADD).then_inc(y_added, 1)

            def ffn(base, s, hid0, gate0, y0, zeros):
                u0, b0 = base
                g0 = u0 // 4

                def gate_up(grp, blk, n, gate, c, added):
                    split(grp + 1)
                    dve.wait_ge(y_added, added)
                    dve.wait_ge(hid_ready, n + 1)
                    fold(4 * grp + 4, 0, tmp[:, 0])
                    split(grp + 2)
                    fold(4 * grp + 8, 1, tmp[:, 1])
                    dve.wait_ge(gate_act, gate + 1)
                    dve.wait_ge(folded, blk + 4)
                    dve.tensor_tensor(tmp[:, 1], tmp[:, 1], tmp[:, 0], MUL).then_inc(h_ready, 1)
                    hidden(n, c, 1)

                with dve.Fori(0, FULL) as q:
                    with dve.Fori(0, 4) as i:
                        gate_up(12 * q + (2 * i + g0), 12 * q + (2 * i + b0), 4 * q + (i + hid0), 4 * q + (i + gate0), i, 4 * q + y0)
                    dve.wait_ge(y_zero, zeros)
                    with dve.Fori(0, 2) as i:
                        for j in range(2):
                            split(12 * q + (2 * i + (g0 + 9 + j)))
                            add_to_y(48 * q + (8 * i + (u0 + 36 + 4 * j)), 12 * q + (2 * i + (b0 + 8 + j)), j, 2 * i + j,
                                     4 * q + (2 * i + (y0 + j)), 4 * q + (hid0 + 5))
                g1, b1, h1, y1 = g0 + 12 * FULL, b0 + 12 * FULL, hid0 + 4 * FULL, y0 + 4 * FULL
                with dve.Fori(0, REST) as i:
                    gate_up(2 * i + g1, 2 * i + b1, i + h1, i + (gate0 + 4 * FULL), i, y1)
                g2, b2 = g1 + 2 * REST, b1 + 2 * REST
                ahead = SLOTS
                for c in range(4):
                    upto = REST * (c + 2) if c < 3 else REST * 4
                    for v in range(ahead, min(upto, REST * 4)):
                        split(g2 + v // SLOTS, [v % SLOTS])
                    ahead = max(ahead, min(upto, REST * 4))
                    if c == 3 and s.n != 5:
                        split(g2 + REST)
                    add_to_y(4 * g2 + REST * (c + 1), b2 + c, c % 2, c, y1 + c, h1 + REST + 1)
                    dve.wait_ge(y_added, y1 + c + 1)
                    dve.tensor_tensor(xr[:, chunk(c), :], xr[:, chunk(c), :], y[:, chunk(c), :], ADD).then_inc(x_new, 1)

            split(0)
            for h in range(2):
                dve.wait_ge(x_rows_tr, h + 1)
                dve.tensor_copy(xr[:, 8 * h:8 * h + 8, :].rearrange("p k t -> p (k t)"),
                                acc[:, 4 * h:4 * h + 4, :].rearrange("p b n -> p (b n)")).then_inc(folded, 1)
            dve.wait_ge(ada_done, KT)
            dve.tensor_tensor(coef[:, 0:KT], ada[:, 0:KT], par[:, cols["mix_post"]:cols["mix_post"] + KT], MUL).then_inc(y_added, 1)
            dve.tensor_tensor(coef[:, 2 * KT:3 * KT], ada[:, 3 * KT:4 * KT], par[:, cols["mlp_post"]:cols["mlp_post"] + KT], MUL).then_inc(hid_ready, 1)
            dve.scalar_tensor_tensor(coef[:, KT:2 * KT], ada[:, 2 * KT:3 * KT], 1.0, par[:, cols["mlp_pre"]:cols["mlp_pre"] + KT],
                                     ADD, MUL).then_inc(coef_ready, 1)
            with dve.Fori(0, 4) as i:
                split(2 * i + 1)
                dve.wait_ge(y_added, i + 1)
                fold(8 * i + 4, 0, tmp[:, 0])
                split(2 * i + 2)
                fold(8 * i + 8, 1, tmp[:, 1])
                dve.wait_ge(gate_act, i + 1)
                dve.tensor_tensor(y[:, chunk(i), :], tmp[:, 0], tmp[:, 1], MUL).then_inc(y_added, 1)
            dve.wait_ge(coef_ready, 1)
            seam(SEAMS[0])
            G = MLP[0] // 4
            with dve.Fori(0, MLP_PARTS) as q:
                with dve.Fori(0, 2) as i:
                    for j in range(2):
                        n = 4 * q + (2 * i + j)
                        split(8 * q + (2 * i + (G + 1 + j)))
                        dve.wait_ge(y_added, 4 * q + Y_MLP)
                        dve.wait_ge(hid_ready, n + 1)
                        fold(32 * q + (8 * i + (MLP[0] + 4 * j + 4)), j, tmp[:, j])
                        dve.wait_ge(folded, 8 * q + (2 * i + (MLP[1] + j + 3)))
                        dve.scalar_tensor_tensor(tmp[:, j], tmp[:, j], 0.0, tmp[:, j], ALU.max, MUL).then_inc(h_ready, 1)
                        hidden(n, 2 * i + j, j)
                dve.wait_ge(y_zero, 1)
                with dve.Fori(0, 2) as i:
                    for j in range(2):
                        split(8 * q + (2 * i + (G + 5 + j)))
                        add_to_y(32 * q + (8 * i + (MLP[0] + 20 + 4 * j)), 8 * q + (2 * i + (MLP[1] + 4 + j)), j, 2 * i + j,
                                 4 * q + (2 * i + (Y_MLP + j)), 4 * q + 5)
            seam(SEAMS[1])
            G = AB_IN[0] // 4

            def convolve(tiles, first, last):
                if first == 0:
                    for k in tiles:
                        dve.tensor_scalar(z[:, k, :], conv_in[:, k, 0:TOK], par[:, cols["dw_w"] + k:cols["dw_w"] + k + 1],
                                          par[:, cols["dw_b"] + k:cols["dw_b"] + k + 1], MUL, ADD).then_inc(conv_dve, 1)
                    first = 1
                before = (4 - CONV_POOL) * W_CONV if tiles[0] > CONV_POOL else 0
                with dve.Fori(first, last) as w:
                    for n, k in enumerate(tiles):
                        x, c = conv_in[:, k, ds(w, TOK)], par[:, ds(8 * w + (cols["dw_w"] + k), 1)]
                        dve.wait_ge(conv_dve, len(tiles) * w + (before + n + 1 - len(tiles)))
                        dve.scalar_tensor_tensor(z[:, k, :], x, c, z[:, k, :], MUL, ADD).then_inc(conv_dve, 1)

            first_half, second_half = range(CONV_POOL, 4), range(4, 8)
            for j in range(8):
                place = (0, 8, 4, 12, 16, 20, 24, 28)[j]
                split(G + 1 + j)
                fold(AB_IN[0] + 4 * j + 4, j % 2, z[:, place:place + 4, :])
                if j == 2:
                    dve.wait_ge(conv_in_ready, 1)
                    dve.wait_ge(pad_zero, 1)
                    convolve(first_half, 0, 16)
                if j == 3:
                    convolve(first_half, 16, W_CONV)
                if j == 4:
                    dve.wait_ge(gate_sig, 2)
                    dve.tensor_tensor(conv_in[:, 4:8, PAD:PAD + TOK], z[:, 4:8, :], z[:, 12:16, :], MUL).then_inc(conv_in2_ready, 1)
                    dve.wait_ge(conv_in2_ready, 1)
                if j >= 4:
                    convolve(second_half, 7 * (j - 4), min(7 * (j - 3), 26))
            convolve(second_half, 26, W_CONV)
            zc, zu, zv = z[:, 0:8, :], z[:, 16:24, :], z[:, 24:32, :]
            flat = "p k t -> p (k t)"
            lower = acc[:, 0:4, :].rearrange("p b n -> p (b n)")

            def wide(v):
                return v.unsqueeze(1).broadcast_to([P, 8, TOK])

            dve.wait_ge(conv_mean, 1)
            dve.scalar_tensor_tensor(zc.rearrange(flat), lower, -1.0 / P, zc.rearrange(flat), MUL, ADD).then_inc(conv_centred, 1)
            dve.wait_ge(v_mean, 1)
            dve.tensor_scalar(rs[:, 1, :], ps[4][:, 0:TOK], 1.0 / (8 * P), None, MUL).then_inc(v_mu, 1)
            dve.wait_ge(v_mu, 1)
            dve.tensor_tensor(zv, zv, wide(rs[:, 1, :]), SUB).then_inc(v_centred, 1)
            dve.wait_ge(conv_var, 1)
            dve.tensor_scalar(conv_sq[:, :, :].rearrange(flat), lower, 1.0 / P, LN_EPS, MUL, ADD).then_inc(conv_ms, 1)
            dve.wait_ge(v_var, 1)
            rsqrt(1, ps[7][:, 0:TOK], 0, v_ms, v_root, v_rs, 8 * P, LN_EPS)
            dve.tensor_tensor(zv, zv, wide(rs[:, 0, :]), MUL).then_inc(v_scaled, 1)
            dve.wait_ge(v_scaled, 1)
            for k in range(8):
                ins = dve.tensor_scalar(z[:, 24 + k, :], z[:, 24 + k, :], par[:, cols["sln_g"] + k:cols["sln_g"] + k + 1],
                                        par[:, cols["sln_b"] + k:cols["sln_b"] + k + 1], MUL, ADD)
            ins.then_inc(v_out, 1)
            dve.wait_ge(conv_root, 1)
            dve.reciprocal(conv_sq[:, :, :], conv_sq[:, :, :]).then_inc(conv_rs, 1)
            dve.wait_ge(conv_rs, 1)
            dve.tensor_tensor(zc, zc, conv_sq[:, :, :], MUL).then_inc(conv_normed, 1)
            for c in range(2):
                dve.wait_ge(mixed, c + 1)
                dve.tensor_tensor(z[:, 16 + CH * c:16 + CH * (c + 1), :].rearrange(flat), z[:, 16 + CH * c:16 + CH * (c + 1), :].rearrange(flat),
                                  acc[:, 4 + 2 * c:6 + 2 * c, :].rearrange("p b n -> p (b n)"), MUL).then_inc(gated, 1)
            for c in range(4):
                dve.wait_ge(xin_hi, X_MIX + c + 1)
                rest(xin, z[:, CH * c:CH * (c + 1), :] if c < 2 else z[:, 8 + CH * c:8 + CH * (c + 1), :], chunk(c), xin_ready)
            G = AB_OUT[0] // 4
            with dve.Fori(0, 2) as i:
                for j in range(2):
                    split(2 * i + (G + 1 + j))
                    dve.wait_ge(x_new, 2 * i + (2 * NCK + j))
                    fold(8 * i + (AB_OUT[0] + 4 * j + 4), j, tmp[:, j])
                    dve.wait_ge(folded, 2 * i + (AB_OUT[1] + j + 3))
                    c = chunk(2 * i + j)
                    dve.tensor_tensor(xr[:, c, :], xr[:, c, :], tmp[:, j], ADD).then_inc(x_new, 1)
            seam(SEAMS[2])
            ffn(FFN0, SEAMS[3], HID0, 4, Y_FFN0, 2)
            seam(SEAMS[3])
            for g in range(9):
                if g < 8:
                    dve.wait_ge(f1_done, g + 1)
                    if g >= 2:
                        dve.wait_ge(f2_done, g - 1)
                    dve.tensor_copy(tmp[:, g % 2].rearrange("p a t -> p (a t)"),
                                    acc[:, 2 * (g % 2):2 * (g % 2) + 2, :].rearrange("p b n -> p (b n)")).then_inc(f1_sb, 1)
                if g:
                    dve.wait_ge(f_hi, g)
                    rest(xin, ps[4 + (g - 1) % 2].rearrange("p (k t) -> p k t", k=2), slice(2 * g - 2, 2 * g), f_lo)
            G = FNET[0] // 4
            dve.wait_ge(f2_done, 8)
            with dve.Fori(0, 2) as i:
                for j in range(2):
                    split(2 * i + (G + 1 + j))
                    dve.wait_ge(x_new, 2 * i + (4 * NCK + j))
                    fold(8 * i + (FNET[0] + 4 * j + 4), j, tmp[:, j])
                    dve.wait_ge(folded, 2 * i + (FNET[1] + j + 3))
                    for k in range(CH):
                        o = xr[:, ds(8 * i + (4 * j + k), 1), :]
                        ins = dve.scalar_tensor_tensor(o, tmp[:, j, k:k + 1, :], par[:, ds(8 * i + (cols["fnet_b"] + 4 * j + k), 1)], o, ADD, ADD)
                    ins.then_inc(x_new, 1)
            seam(SEAMS[4])
            ffn(FFN1, SEAMS[5], HID1, 4 + HID1 - HID0, Y_FFN1, 3)
            seam(SEAMS[5])

        def GEMM_POOL(pool):
            yflat = y[:, :, :].rearrange("p k t -> p (k t)")
            pool.wait_ge(x_new, NCK)
            pool.memset(yflat, 0.0).then_inc(y_zero, 1)
            pool.wait_ge(x_new, 2 * NCK)
            pool.memset(conv_in[:, :, 0:PAD], 0.0)
            pool.memset(conv_in[:, :, PAD + TOK:], 0.0).then_inc(pad_zero, 1)
            pool.wait_ge(gate_sig, 1)
            pool.tensor_tensor(conv_in[:, 0:4, PAD:PAD + TOK], z[:, 0:4, :], z[:, 8:12, :], ALU.mult).then_inc(conv_in_ready, 1)
            pool.wait_ge(pad_zero, 1)
            pool.wait_ge(conv_in_ready, 1)
            step = 0
            for w in range(W_CONV):
                for k in range(CONV_POOL):
                    x, c = conv_in[:, k, w:w + TOK], par[:, cols["dw_w"] + 8 * w + k:cols["dw_w"] + 8 * w + k + 1]
                    if w == 0:
                        pool.tensor_scalar(z[:, k, :], x, c, par[:, cols["dw_b"] + k:cols["dw_b"] + k + 1],
                                           ALU.mult, ALU.add).then_inc(conv_pool, 1)
                    else:
                        pool.wait_ge(conv_pool, step - 1)
                        pool.tensor_scalar(conv_tmp[:, step % 2, :], x, c, None, ALU.mult).then_inc(conv_mul, 1)
                        pool.wait_ge(conv_mul, step + 1 - CONV_POOL)
                        pool.tensor_tensor(z[:, k, :], z[:, k, :], conv_tmp[:, step % 2, :], ALU.add).then_inc(conv_pool, 1)
                    step += 1
            pool.wait_ge(xin_ready, X_MIX + NCK)
            pool.memset(yflat, 0.0).then_inc(y_zero, 1)
            pool.wait_ge(f_lo, 8)
            pool.memset(yflat, 0.0).then_inc(y_zero, 1)

        block = ctx.enter_context(nc.Block())

        def s5_loop(eng, tile):
            tile(0, 0, KT - 1, False)
            tile(1, 1, KT - 2, True)
            with eng.Fori(1, KT // 2 - 2) as i:
                tile(2 * i, 0, KT, True)
                tile(2 * i + 1, 1, KT, True)
            for k in range(KT - 4, KT):
                tile(k, k % 2, KT - 1 - k, True)

        @block.sync
        def _(sp):
            sp.dma_start(consts[:, :], a["c_main"]).then_inc(const_in, 16)
            sp.dma_start(crow[0:KT, :], rows(a["c_ctx"])).then_inc(const_in, 16)
            sp.dma_start(crow[KT:2 * KT, :], rows(a["c"][0])).then_inc(const_in, 16)
            for n, v in enumerate([a["s5_a_re"], a["s5_a_im"]]):
                sp.dma_start(arow[:, n, :], v[0].rearrange("d (q s) p -> (d q) (s p)", s=2)).then_inc(s5p_in, 16)
            sp.dma_start(ldt[:, :], a["s5_log_dt"][0].rearrange("d (q s) -> (d q) s", s=2)).then_inc(s5p_in, 16)
            sp.dma_start(s5c[:, :], a["c_s5"]).then_inc(s5p_in, 16)
            for ri in range(2):
                sp.dma_start(braw[:, ri, :, :], b_view[ri]).then_inc(s5p_in, 16)
            for t, r, k, v in par_dma:
                sp.dma_start(prows[r:r + k, t, :], v).then_inc(const_in, 16)
            sp.dma_start(bmod_row[:, :], a["b_mod"][0:1, 0:2 * D].broadcast_to([64, 2 * D])).then_inc(rows_in, 16)
            sp.dma_start(gain_row[:, :], a["norm_mix_pre"].broadcast_to([64, D])).then_inc(rows_in, 16)
            def ada_units(u0, col, first=False):
                for k in range(UK):
                    if not first:
                        sp.wait_ge(ada_unit, u0 + (k + 1 - SLOTS))
                    sp.dma_start(raw[:, k, :, :], w_mod[:, k * UK:(k + 1) * UK, ds(col, UN)]).then_inc(raw_ready[k], 16)

            ada_units(0, D, first=True)
            for n, v in enumerate([ctx2[0:P], ctx2[P:], x2[0:P], x2[P:]]):
                if n:
                    sp.wait_ge(xstat_sq, n)
                sp.dma_start(xstat[:, :], v).then_inc(xstat_in, 16)
            for ri in range(2):
                sp.dma_start(craw[:, ri, :, :], c_view[ri][0]).then_inc(c_tile, 16)
            sp.wait_ge(xstat_sq, 4)
            sp.dma_start(ss_dram.rearrange("(n p) -> p n", p=P), ss_sb[:, :], allow_slow_non_contiguous=True).then_inc(ss_out, 16)
            sp.wait_ge(ss_out, 16)
            sp.dma_start(rstd_x[:, :], ss_dram.rearrange("(c j) -> c j", j=L)).then_inc(ss_in, 16)
            for s in range(2):
                sp.dma_start(xc[s * NCH:(s + 1) * NCH, :, :], xch[s][:, :, 0:P]).then_inc(x_tile, 16)

            ada_units(4, 0)
            for b in range(1, 4):
                ada_units(8 * b, b * UN + D)
                ada_units(8 * b + 4, b * UN)

            def load_c(n):
                for ri in range(2):
                    sp.dma_start(craw[:, ri, :, :], c_view[ri][n]).then_inc(c_tile, 16)

            def load_x(n):
                for s in range(2):
                    sp.dma_start(xc[s * NCH:(s + 1) * NCH, :, :], xch[s][:, :, ds(n * P, P)]).then_inc(x_tile, 16)

            def toeplitz(n, first=False):
                if not first:
                    sp.wait_ge(t_in, 16 * L * n)
                sp.wait_ge(r_sb, n + 1)
                sp.dma_start(r_dram.rearrange("g h m -> (g h) m"), rw[:, :]).then_inc(r_out, 16)
                sp.wait_ge(r_out, 16 * (n + 1))
                if not first:
                    sp.wait_ge(y_done, n)
                for j in range(L):
                    sp.dma_start(tw[j * GRP:(j + 1) * GRP, :, :],
                                 r_dram[:, :, (L - 1 - j) * GRP:(2 * L - 1 - j) * GRP].rearrange("g h m -> h g m")
                                 ).then_inc(t_in, 16)

            sp.wait_ge(c_sel, 1)
            load_c(1)
            toeplitz(0, first=True)
            ada_units(32, 2 * D)
            sp.wait_ge(xt_scaled, 1)
            load_x(1)
            sp.wait_ge(c_sel, 2)
            load_c(2)

            def tile(k, _, left, before):
                if left >= 2:
                    sp.wait_ge(xt_scaled, k + 2)
                    load_x(k + 2)
                if left >= 1:
                    ada_units(4 * k + 36, (k + 1) * UN + 2 * D)
                if left >= 3:
                    sp.wait_ge(c_sel, k + 3)
                    load_c(k + 3)
                if left >= 1:
                    toeplitz(k + 1)

            s5_loop(sp, tile)
            sp.wait_ge(r_out, 16 * KT)
            sp.wait_ge(ss_out, 16)
            GEMM_SP(sp)

        @block.tensor
        def _(pe):
            pe.wait_ge(const_in, 16 * (3 + len(par_dma)))
            pe.wait_ge(cond_silu, 1)
            pe.transpose(ps[0][:, 0:2 * KT], crow[:, :], ident[0:2 * KT, 0:2 * KT]).then_inc(cond_tr, 1)
            for t in range(4):
                pe.transpose(ps[1][:, t * P:(t + 1) * P], prows[:, t, :], ident).then_inc(par_tr, 1)
            pe.wait_ge(s5p_in, 16 * 6)
            pe.wait_ge(ldt_wide, 1)
            for n in range(3):
                pe.transpose(ps[2][:, n * P:(n + 1) * P], arow[:, n, :], ident).then_inc(a_tr, 1)
            def ada1_block(m, bank, units):
                for k in range(UK):
                    pe.wait_ge(raw_ready[k], 16 * (m + 1))
                    for q in range(UK):
                        ins = pe.matmul(bank[0:64, :], cond[:, k * UK + q, :], raw[:, k, q, :],
                                        start=(k + q == 0), stop=(k == UK - 1 and q == UK - 1))
                    ins.then_inc(ada_unit, 1)

            def ada1_pair(b, first=False):
                for half, bank in ((0, ps[0]), (1, ps[7])):
                    if not first:
                        pe.wait_ge(ada1_sb, 2 * b + half - 1)
                    ada1_block(2 * b + half, bank, None)


            for n, (ri, d) in enumerate([(0, 0), (1, 0), (0, 1), (1, 1)]):
                lo = 3 + 2 * (n % 2)
                if n == 2:
                    pe.wait_ge(cond_ready, 1)
                    ada1_pair(0, first=True)
                if n >= 2:
                    pe.wait_ge(b_sb, n - 1)
                for h in range(GRP):
                    bank = ps[lo + h // 8]
                    for s in range(2):
                        ins = pe.matmul(bank[s * NST:(s + 1) * NST, (h % 8) * 64:(h % 8 + 1) * 64],
                                        braw[:, ri, d, h:NST * GRP:GRP], sel_g[:, s * 64:(s + 1) * 64], start=True, stop=True)
                ins.then_inc(b_sel, 1)
            def select_c(n):
                pe.wait_ge(c_tile, 32 * (n + 1))
                for ri in range(2):
                    for d in range(2):
                        for s in range(2):
                            ins = pe.matmul(ps[5][s * NST:(s + 1) * NST, 256 + (2 * ri + d) * 64:256 + (2 * ri + d + 1) * 64],
                                            craw[:, ri, d, :], sel_c[:, s * 64:(s + 1) * 64], start=True, stop=True)
                ins.then_inc(c_sel, 1)

            pe.wait_ge(b_sb, 4)
            select_c(0)
            with pe.Fori(1, 3) as b:
                ada1_pair(b)

            def transpose_e(n):
                pe.wait_ge(bpow_done, n + 1)
                if not isinstance(n, int) or n > 0:
                    pe.wait_ge(e_sb, 4 * n)
                for q in range(4):
                    if q >= 2:
                        pe.wait_ge(e_sb, 4 * n + q - 1)
                    for r in range(4):
                        ri, cb = divmod(4 * q + r, CB)
                        ins = pe.transpose(ps[3 + q % 2][:, r * P:(r + 1) * P], bpow[:, ri, cb, :], ident)
                    ins.then_inc(e_tr, 1)

            def lag_blocks(n, buf):
                pe.wait_ge(cpow_done, n + 1)
                pe.wait_ge(bd_sb, n + 1)
                for kp in range(GT // 2):
                    for d in range(2):
                        win, to = ((0, 112), (GRP, 0))[d]
                        for ri in range(2):
                            ins = pe.matmul(ps[5][32 * kp:32 * kp + 32, to:to + P],
                                            bd[:, 4 * d + kp, ri, :, :].rearrange("p s h -> p (s h)"),
                                            buf[:, ri, 4 * d + kp, win:win + P],
                                            start=(d + ri == 0), stop=(d + ri == 2), skip_group_check=True)
                ins.then_inc(k_done, 1)

            transpose_e(0)
            lag_blocks(0, cpow[0])
            ada1_pair(3)
            pe.wait_ge(c_sb, 1)
            pe.wait_ge(r_sb, 1)
            select_c(1)

            def output_transposes(n):
                pe.wait_ge(y_gelu, n + 1)
                if isinstance(n, int) and n == 0:
                    pe.wait_ge(zt_zero, 1)
                else:
                    pe.wait_ge(z_lo, n)
                for i in range(L):
                    ins = pe.matmul(ps[7][:, 256 + i * NCH:256 + (i + 1) * NCH], zt[:, i, :], eye_c, start=True, stop=True)
                ins.then_inc(z_tr, 1)

            def tile(k, b, left, before):
                pe.wait_ge(xt_done, k + 1)
                for g in range(GT):
                    ins = pe.matmul(ps[6][:, g * 64:(g + 1) * 64], xt[:, g, :, :].rearrange("c j h -> c (j h)"), ident[0:64, 0:64],
                                    start=True, stop=True)
                ins.then_inc(u_tr, 1)
                pe.wait_ge(u_sb, k + 1)
                if before:
                    pe.wait_ge(y_gelu, k)
                pe.wait_ge(e_sb, 4 * (k + 1))
                for ri in range(2):
                    for cb in range(CB):
                        d, kp = divmod(cb, GT // 2)
                        for s in range(2):
                            uv = u[:, 2 * kp + s, :].rearrange("p (q c) -> p q c", q=2)
                            ins = pe.matmul(ps[1 + ri][s * NST:(s + 1) * NST, cb * 64:(cb + 1) * 64],
                                            ew[:, ri, cb, s * NST:(s + 1) * NST], uv[:, :, ::-1] if d else uv, start=True, stop=True)
                ins.then_inc(v_done, 1)
                if before:
                    output_transposes(k - 1)
                if before:
                    pe.wait_ge(ada_sb, k)
                else:
                    pe.wait_ge(ada1_sb, 8)
                for kk in range(UK):
                    pe.wait_ge(raw_ready[kk], 16 * (k + 9))
                    for q in range(UK):
                        ins = pe.matmul(ps[0][32 * q:32 * q + 32, :], cond[:, kk * UK + q, 32:64], raw[:, kk, q, :],
                                        start=(kk == 0), stop=(kk == UK - 1))
                    ins.then_inc(ada_unit, 1)
                if left >= 1:
                    transpose_e(k + 1)
                if left >= 2:
                    pe.wait_ge(c_sb, k + 2)
                    pe.wait_ge(r_sb, k + 1)
                    select_c(k + 2)
                pe.wait_ge(s_done, k + 1)
                pe.wait_ge(t_in, 16 * L * (k + 1))
                for half in range(2):
                    for term in range(5):
                        for q in range(4):
                            g = 4 * half + q
                            kp, s = divmod(g, 2)
                            o = ps[1][32 * q:32 * q + NCH, half * P:(half + 1) * P]
                            if term == 0:
                                ins = pe.matmul(o, u[:, g, NCH:2 * NCH], tw[:, g, :], start=True, stop=False)
                                continue
                            d, ri = divmod(term - 1, 2)
                            w = GRP * (1 - d)
                            ins = pe.matmul(o, st[s * NST:(s + 1) * NST, ri, 4 * d + kp, :], cpow[b][s * NST:(s + 1) * NST, ri, 4 * d + kp, w:w + P],
                                            start=False, stop=(term == 4))
                ins.then_inc(y_done, 1)
                if left >= 1:
                    pe.wait_ge(r_sb, k + 1)
                    pe.wait_ge(c_sb, k + (3 if left >= 2 else 2))
                    lag_blocks(k + 1, cpow[1 - b])
                pe.wait_ge(ada_sb, k + 1)
                if before:
                    pe.wait_ge(z_lo, k)
                for r in range(NT):
                    ins = pe.matmul(ps[7][:, r:r + 1], adarow[:, r * P:(r + 1) * P], quad, start=True, stop=True)
                ins.then_inc(ada_col, 1)

            s5_loop(pe, tile)
            output_transposes(KT - 1)
            GEMM_PE(pe)

        @block.scalar
        def _(act):
            act.wait_ge(const_in, 16 * (3 + len(par_dma)))
            act.activation(crow[:, :], crow[:, :], ACT.Silu).then_inc(cond_silu, 1)
            def copy_c(n):
                act.activation(ct[:, 0, :, :].rearrange("p b h -> p (b h)"), ps[5][:, 256:384], ACT.Copy)
                act.activation(ct[:, 1, :, :].rearrange("p b h -> p (b h)"), ps[5][:, 384:512], ACT.Copy,
                               scale=-1.0).then_inc(c_sb, 1)

            act.wait_ge(angle_ready, 1)
            act.activation(tv[4][:, :], tv[4][:, :], ACT.Sin)
            act.activation(tv[5][:, :], tv[5][:, :], ACT.Sin).then_inc(sin_ready, 1)
            for n in range(4):
                act.wait_ge(xstat_in, 16 * (n + 1))
                act.activation(xstat[:, :], xstat[:, :], ACT.Square, accum_out=ss_sb[:, n:n + 1]).then_inc(xstat_sq, 1)
            act.wait_ge(c_sel, 1)
            copy_c(0)

            def ada1_copy(b):
                for half, bank in ((0, ps[0]), (1, ps[7])):
                    act.wait_ge(ada_unit, 8 * b + 4 * half + 4)
                    act.activation(sb[:, half, ds(b * UN, UN)], bank[0:64, :], ACT.Copy).then_inc(ada1_sb, 1)

            with act.Fori(0, 3) as b:
                ada1_copy(b)

            def block_diagonal_b(n):
                for s in range(2):
                    r = slice(s * NST, (s + 1) * NST)
                    ins = act.activation(bd[r, :, :, s, :].rearrange("p b r h -> p r b h"), bb[r, :, ds(n * CB, CB), :], ACT.Copy)
                ins.then_inc(bd_sb, 1)

            def copy_e(n):
                for q in range(4):
                    act.wait_ge(e_tr, 4 * n + q + 1)
                    act.activation(ew[:, :, :, :].rearrange("p r b m -> p (r b m)")[:, q * 512:(q + 1) * 512],
                                   ps[3 + q % 2][:, :], ACT.Copy).then_inc(e_sb, 1)

            def normalise_x(n):
                act.wait_ge(x_tile, 32 * (n + 1))
                for j in range(L):
                    ins = act.activation(xt[:, :, j, :], xc[:, j, :].rearrange("c (g h) -> c g h", g=GT), ACT.Copy,
                                         scale=rstd_x[:, j:j + 1])
                ins.then_inc(xt_scaled, 1)

            act.wait_ge(tables_ready, 1)
            block_diagonal_b(0)
            copy_e(0)
            ada1_copy(3)
            act.wait_ge(c_sel, 2)
            act.wait_ge(cpow_done, 1)
            copy_c(1)
            act.wait_ge(k_done, 1)
            block_diagonal_b(1)
            act.wait_ge(ss_ready, 1)
            act.activation(rstd_x[:, :], rstd_x[:, :], ACT.Sqrt).then_inc(rstd_root, 1)
            act.wait_ge(rstd_ready, 1)
            normalise_x(0)

            def copy_output(n):
                act.wait_ge(z_tr, n + 1)
                act.activation(xin[:, ds(n, 1), 0:TOK].rearrange("p o (c i) -> p (o i) c", i=L),
                               ps[7][:, 256:512].rearrange("p (i c) -> p i c", i=L), ACT.Copy).then_inc(z_hi, 1)

            def tile(k, b, left, before):
                act.wait_ge(u_tr, k + 1)
                if before:
                    act.wait_ge(y_done, k)
                act.activation(u[:, :, :].rearrange("p g c -> p (g c)"), ps[6][:, :], ACT.Copy).then_inc(u_sb, 1)
                if left >= 1:
                    normalise_x(k + 1)
                if before:
                    copy_output(k - 1)
                act.wait_ge(ada_unit, 32 + 4 * (k + 1))
                if before:
                    act.wait_ge(ada_col, k)
                act.activation(adarow[:, :], ps[0][:, :], ACT.Copy).then_inc(ada_sb, 1)
                if left >= 1:
                    act.wait_ge(v_done, k + 1)
                    copy_e(k + 1)
                if left >= 2:
                    act.wait_ge(c_sel, k + 3)
                    act.wait_ge(cpow_done, k + 2)
                    copy_c(k + 2)
                act.wait_ge(y_done, k + 1)
                if isinstance(k, int) and k == 0:
                    act.wait_ge(zt_zero, 1)
                if before:
                    act.wait_ge(z_tr, k)
                for q in range(4):
                    r = slice(32 * q, 32 * q + NCH)
                    ins = act.activation(zt[r, :, :].rearrange("c i (f q h) -> c f i q h", f=2, q=4)[:, :, :, q],
                                         ps[1][r, 0:2 * P].rearrange("c (f i h) -> c f i h", f=2, i=L), ACT.Gelu_apprx_tanh)
                ins.then_inc(y_gelu, 1)
                if left >= 2:
                    act.wait_ge(k_done, k + 2)
                    block_diagonal_b(k + 2)

            s5_loop(act, tile)
            copy_output(KT - 1)
            GEMM_ACT(act)

        @block.vector
        def _(dve):
            def tt(o, x, y, op):
                return dve.tensor_tensor(o, x, y, op)

            MUL, ADD, SUB = ALU.mult, ALU.add, ALU.subtract

            def cmul(c, o, x, y, t, done=None):
                c.settle()
                c(tt(o[0], x[0], y[0], MUL))
                c(tt(t[0], x[1], y[1], MUL))
                c(tt(o[1], x[0], y[1], MUL))
                c(tt(t[1], x[1], y[0], MUL))
                c.settle()
                c(tt(o[0], o[0], t[0], SUB))
                last = tt(o[1], o[1], t[1], ADD)
                if done is None:
                    c(last)
                else:
                    last.then_inc(done, 1)

            c = Chain(dve, prep)
            dve.wait_ge(cond_tr, 1)
            for s in range(2):
                ins = dve.tensor_copy(cond[:, :, 32 * s:32 * s + 32], ps[0][:, s * KT:(s + 1) * KT].unsqueeze(2).broadcast_to([P, KT, 32]))
            ins.then_inc(cond_ready, 1)
            dve.wait_ge(s5p_in, 16 * 6)
            dve.tensor_copy(arow[:, 2, :].rearrange("r (s p) -> r s p", s=2),
                            ldt[:, :].unsqueeze(2).broadcast_to([P, 2, NST])).then_inc(ldt_wide, 1)
            dve.wait_ge(par_tr, 4)
            c(dve.tensor_copy(par[:, :], ps[1][:, :]))
            dve.wait_ge(a_tr, 3)
            for n in range(3):
                c(dve.tensor_copy(tv[n][:, :].rearrange("p (k d q) -> p d k q", k=KT, d=2),
                                  ps[2][:, n * P:(n + 1) * P].rearrange("p (d k q) -> p d k q", d=2, k=KT)))
            T = [t[:, :] for t in tv]
            are, aim = T[0], T[1]
            MAGIC = 1.5 * 2.0 ** 23

            def exp(o, x, t, ti):
                c.settle()
                c(dve.tensor_scalar(t[0], x, 1.4426950408889634, MAGIC, MUL, ADD))
                c.settle()
                c(dve.tensor_scalar(t[0], t[0], MAGIC, -126.0, SUB, ALU.max))
                c.settle()
                c(dve.tensor_scalar(t[0], t[0], 127.0, None, ALU.min))
                c.settle()
                c(dve.scalar_tensor_tensor(t[1], t[0], -0.693359375, x, MUL, ADD))
                c(dve.tensor_scalar(ti, t[0], 127.0, 2.0 ** 23, ADD, MUL))
                c.settle()
                c(dve.scalar_tensor_tensor(t[1], t[0], 2.12194440e-4, t[1], MUL, ADD))
                c.settle()
                c(dve.tensor_scalar(t[2], t[1], 1.0 / 5040, None, MUL))
                for f in (720, 120, 24, 6, 2, 1):
                    c.settle()
                    c(dve.scalar_tensor_tensor(t[2], t[2], 1.0 / f, t[1], ADD, MUL))
                c.settle()
                c(dve.scalar_tensor_tensor(o, t[2], 1.0, ti.bitcast(F32), ADD, MUL))

            ti = tv[23][:, :].bitcast(I32)
            dt, x, th, mag = T[2], T[3], T[6], T[7]
            exp(dt, T[2], T[8:11], ti)
            c.settle()
            c(tt(x, are, dt, MUL))
            c(tt(th, aim, dt, MUL))
            exp(mag, x, T[8:11], ti)
            c(dve.tensor_scalar(T[8], th, 0.15915494309189535, MAGIC, MUL, ADD))
            c.settle()
            c(dve.tensor_scalar(T[8], T[8], MAGIC, None, SUB))
            for n, part in enumerate((6.28125, 1.93500518798828125e-3, 3.019915981956753e-7)):
                c.settle()
                c(dve.scalar_tensor_tensor(T[4], T[8], -part, th if n == 0 else T[4], MUL, ADD))
            c.settle()
            c(dve.tensor_scalar(T[9], T[4], float(np.pi / 2), -2 * float(np.pi), ALU.is_gt, MUL))
            c.settle()
            c(dve.scalar_tensor_tensor(T[5], T[4], float(np.pi / 2), T[9], ADD, ADD))
            c.settle()
            LIM = 3.1415925
            c(dve.tensor_scalar(T[4], T[4], LIM, -LIM, ALU.min, ALU.max))
            dve.tensor_scalar(T[5], T[5], LIM, -LIM, ALU.min, ALU.max).then_inc(angle_ready, 1)
            dve.wait_ge(sin_ready, 1)
            sn, cs = T[4], T[5]
            lam = [T[10], T[11]]
            c(tt(lam[0], mag, cs, MUL))
            c(tt(lam[1], mag, sn, MUL))
            uu, un = [T[12], T[13]], [T[14], T[15]]
            cmul(c, uu, [cs, sn], [cs, sn], T[16:18])
            c.settle()
            cmul(c, un, uu, uu, T[16:18])
            c.settle()
            cmul(c, uu, un, un, T[16:18])
            c.settle()
            c(tt(T[16], uu[0], uu[0], MUL))
            c(tt(T[17], uu[1], uu[1], MUL))
            c(tt(T[18], mag, mag, MUL))
            c.settle()
            c(tt(T[16], T[16], T[17], ADD))
            c(tt(T[18], T[18], T[18], MUL))
            c.settle()
            c(dve.tensor_scalar(T[16], T[16], -0.5, 1.5, MUL, ADD))
            c(tt(r8all[:, :], T[18], T[18], MUL))
            c.settle()
            c(tt(uu[0], uu[0], T[16], MUL))
            c(tt(uu[1], uu[1], T[16], MUL))
            c.settle()
            c(dve.tensor_scalar(T[14], lam[0], 1.0, None, SUB))
            c(tt(T[16], are, are, MUL))
            c(tt(T[17], aim, aim, MUL))
            c.settle()
            c(tt(T[16], T[16], T[17], ADD))
            c(tt(T[18], T[14], are, MUL))
            c(tt(T[19], lam[1], aim, MUL))
            c(tt(T[20], lam[1], are, MUL))
            c(tt(T[21], T[14], aim, MUL))
            c.settle()
            c(dve.reciprocal(T[16], T[16]))
            c(tt(T[18], T[18], T[19], ADD))
            c(tt(T[20], T[20], T[21], SUB))
            c.settle()
            c(tt(T[18], T[18], T[16], MUL))
            c(tt(T[20], T[20], T[16], MUL))
            for n, (ri, d) in enumerate([(0, 0), (1, 0), (0, 1), (1, 1)]):
                dve.wait_ge(b_sel, n + 1)
                for half in range(2):
                    o = bb[:, ri, :, half * 8:half * 8 + 8].rearrange("p (k d q) h -> p k d q h", k=KT, d=2)[:, :, d]
                    i_ = ps[3 + 2 * (n % 2) + half][:, :].rearrange("p (h k q) -> p k q h", h=8, k=KT)
                    ins = dve.tensor_copy(o, i_)
                ins.then_inc(b_sb, 1)
            dve.wait_ge(b_sb, 4)
            wide = [v.unsqueeze(2).broadcast_to([P, NCB, GRP]) for v in (T[18], T[20])]
            c.settle()
            c(tt(btmp[:, 0], bb[:, 0], wide[1], MUL))
            c(tt(btmp[:, 1], bb[:, 1], wide[1], MUL))
            c.settle()
            for ri in range(2):
                c(tt(bb[:, ri], bb[:, ri], wide[0], MUL))
            c.settle()
            c(tt(bb[:, 0], bb[:, 0], btmp[:, 1], SUB))
            c(tt(bb[:, 1], bb[:, 1], btmp[:, 0], ADD))
            c.settle()

            def powers(tab, w, n):
                c(dve.memset(tab[0][:, :, 0:1], 1.0))
                c(dve.memset(tab[1][:, :, 0:1], 0.0))
                for ri in range(2):
                    c(dve.tensor_copy(tab[ri][:, :, 1:2], w[ri].unsqueeze(2)))
                have = 2
                while have < n:
                    k = min(have - 1, n - have)
                    c.settle()
                    cmul(c, [t[:, :, have:have + k] for t in tab], [t[:, :, 1:1 + k] for t in tab],
                         [t[:, :, have - 1:have].broadcast_to([P, NCB, k]) for t in tab], [lpt[:, r, :, 0:k] for r in range(2)])
                    have += k
                c.settle()

            powers([lpa[:, 0], lpa[:, 1]], lam, POW)
            for ri in range(2):
                v = lp[:, ri].rearrange("p (k d q) m -> p k d q m", k=KT, d=2)
                w = lpa[:, ri].rearrange("p (k d q) m -> p k d q m", k=KT, d=2)
                c(dve.tensor_copy(v[:, :, 0], w[:, :, 0]))
                c(dve.tensor_copy(v[:, :, 1], w[:, :, 1, :, ::-1]))
            powers([ab[:, 2], ab[:, 3]], uu, L)
            cmul(c, un, [ab[:, 2, :, L - 1], ab[:, 3, :, L - 1]], uu, T[16:18])
            c.settle()
            powers([ab[:, 0], ab[:, 1]], un, L)
            c(dve.memset(bd[:, :, :, :, :].rearrange("p b r s h -> p (b r s h)"), 0.0))
            c.settle()
            dve.tensor_copy(T[0], T[1]).then_inc(tables_ready, 1)

            mzf = [mz[:, ri].rearrange("p b n -> p (b n)") for ri in range(2)]

            def powers_of_b(c, n):
                for d in range(2):
                    o = [bpow[:, ri, 4 * d:4 * d + 4, :].rearrange("p b (j h) -> p b j h", j=L)[:, :, ::-1] for ri in range(2)]
                    t = [mz[:, ri].rearrange("p b n -> p (b n)").rearrange("p (b j h) -> p b j h", b=4, j=L) for ri in range(2)]
                    pw = []
                    for ri in range(2):
                        v = lp[:, ri, ds(n * CB + 4 * d, 4), d:d + L]
                        pw.append(v.unsqueeze(3).broadcast_to([P, 4, L, GRP]))
                    bv = [bb[:, ri, ds(n * CB + 4 * d, 4), :].unsqueeze(2).broadcast_to([P, 4, L, GRP]) for ri in range(2)]
                    cmul(c, o, pw, bv, t, bpow_done if d else None)

            def phases(c, n):
                a_, b_ = [[ab[:, 2 * w + ri, ds(n * CB, CB), :] for ri in range(2)] for w in range(2)]
                a_ = [v.unsqueeze(3).broadcast_to([P, CB, L, L]) for v in a_]
                b_ = [v.unsqueeze(2).broadcast_to([P, CB, L, L]) for v in b_]
                v4 = lambda w: [w[:, ri].rearrange("p b (x y) -> p b x y", x=L) for ri in range(2)]
                cmul(c, v4(pt), a_, b_, v4(mz))
                c(tt(r8[:, :, :], r8all[:, ds(n * CB, CB)].unsqueeze(2).broadcast_to([P, CB, 2 * NCH]),
                     mask.unsqueeze(1).broadcast_to([P, CB, 2 * NCH]), MUL))
                c.settle()

            def copy_lags(c, n):
                dve.wait_ge(k_done, n + 1)
                c(dve.tensor_copy(rw[:, :], ps[5][:, 0:15 * GRP]))
                c.settle()
                mid = rw[:, 7 * GRP:8 * GRP]
                dve.scalar_tensor_tensor(mid, eye, par[:, ds(n + cols["s5_d"], 1)], mid, MUL, ADD).then_inc(r_sb, 1)

            c0 = Chain(dve, dve_step)
            dve.wait_ge(tables_ready, 1)
            powers_of_b(c0, 0)
            dve.wait_ge(bpow_done, 1)
            phases(c0, 0)
            dve.wait_ge(ss_in, 16)
            dve.tensor_scalar(rstd_x[:, :], rstd_x[:, :], 1.0 / D, EPS, MUL, ADD).then_inc(ss_ready, 1)
            copy_lags(c0, 0)
            dve.wait_ge(rstd_root, 1)
            dve.reciprocal(rstd_x[:, :], rstd_x[:, :]).then_inc(rstd_ready, 1)
            first_steps, tile_steps = c0.n, 34

            def finish(n):
                dve.wait_ge(ada_col, n + 1)
                dve.wait_ge(z_hi, n + 1)
                tt(ada[:, ds(n * NT, NT)], ps[7][:, 0:NT], par[:, ds(n * NT, NT)], ADD).then_inc(ada_done, 1)
                vw = lambda v: v.rearrange("p o (c i) -> p (o i) c", i=L)
                tt(vw(xin[:, ds(n, 1), TOK:2 * TOK]), ps[7][:, 256:512].rearrange("p (i c) -> p i c", i=L),
                   vw(xin[:, ds(n, 1), 0:TOK].bitcast(F32)), SUB).then_inc(z_lo, 1)

            def tile(k, b, left, before):
                c = Chain(dve, dve_step, first_steps + k * tile_steps)
                if left >= 1:
                    dve.wait_ge(e_tr, 4 * (k + 1))
                    powers_of_b(c, k + 1)
                    dve.wait_ge(bpow_done, k + 2)
                dve.wait_ge(v_done, k + 1)
                vr, vi = ps[1][:, :], ps[2][:, :]
                co, si = [pt[:, ri].rearrange("p b n -> p (b n)") for ri in range(2)]
                c(tt(mzf[0], vr, co, MUL))
                c(tt(mzf[1], vi, co, MUL))
                c.settle()
                c(tt(vi, vi, si, MUL))
                c(tt(vr, vr, si, MUL))
                c.settle()
                c(tt(mzf[0], mzf[0], vi, ADD))
                c(tt(mzf[1], mzf[1], vr, SUB))
                c.settle()
                for ri in range(2):
                    c(dve.tensor_tensor_scan(mzf[ri], r8[:, :, :].rearrange("p b n -> p (b n)"), mzf[ri], 0.0, MUL, ADD))
                c.settle()
                if before:
                    dve.wait_ge(y_done, k)
                z = [mz[:, ri, :, NCH - 1:2 * NCH - 1] for ri in range(2)]
                w = [pt[:, ri, :, NCH - 1:2 * NCH - 1] for ri in range(2)]
                t = [ps[1 + ri].rearrange("p (b n) -> p b n", b=CB)[:, :, 0:NCH] for ri in range(2)]
                sx = [turned[:, ri, :, :] for ri in range(2)]
                c(tt(sx[0], z[0], w[0], MUL))
                c(tt(t[0], z[1], w[1], MUL))
                c(tt(sx[1], z[0], w[1], MUL))
                c(tt(t[1], z[1], w[0], MUL))
                c.settle()
                for d in range(2):
                    h = slice(4 * d, 4 * d + 4)
                    for ri in range(2):
                        o = st[:, ri, h, :]
                        ins = tt(o[:, :, ::-1] if d else o, sx[ri][:, h], t[ri][:, h], (SUB, ADD)[ri])
                        ins.then_inc(s_done, 1) if d + ri == 2 else c(ins)
                if left >= 1:
                    dve.wait_ge(s_done, k + 1)
                    phases(c, k + 1)
                if before:
                    finish(k - 1)
                if left >= 1:
                    dve.wait_ge(r_out, 16 * (k + 1))
                    copy_lags(c, k + 1)
                    assert c.n == tile_steps, c.n

            s5_loop(dve, tile)
            finish(KT - 1)
            GEMM_DVE(dve)

        @block.gpsimd
        def _(pool):
            def tt(o, x, y, op):
                return pool.tensor_tensor(o, x, y, op)

            MUL, ADD, SUB = ALU.mult, ALU.add, ALU.subtract

            def powers_of_c(c, n, buf):
                def pw(ri, flat=False):
                    v = lp[:, :, :, :].rearrange("p r b m -> p (r b) m")[:, ds(n * CB + NCB * ri, CB), :] if flat else lp[:, ri, ds(n * CB, CB), :]
                    return v.unsqueeze(3).broadcast_to([P, CB, POW, GRP])

                def cv(ri):
                    return ct[:, ri].unsqueeze(2).broadcast_to([P, CB, POW, GRP])
                o = [buf[:, ri].rearrange("p b (m h) -> p b m h", m=POW) for ri in range(2)]
                t = ptmp[:, :, :].rearrange("p b (m h) -> p b m h", m=POW)
                for ri in range(2):
                    c(tt(t, cv(1 - ri), pw(1, flat=ri == 1), MUL))
                    c(tt(o[ri], cv(ri), pw(0), MUL))
                    c.settle()
                    ins = tt(o[ri], o[ri], t, (ADD, SUB)[ri])
                    if ri == 0:
                        c(ins)
                        c.settle()
                ins.then_inc(cpow_done, 1)

            def modulation(n, r):
                v = sb[:, :, :].rearrange("c r d -> c (r d)")[:, ds(n * P + r * D, P)]
                return v.rearrange("c (g h) -> c g h", g=GT).unsqueeze(1).broadcast_to([64, L, GT, GRP])

            xt_tok = xt[:, :, :, :].rearrange("c g j h -> c j g h")

            def scale(c, n):
                pool.wait_ge(xt_scaled, n + 1)
                c(tt(xt_tok, xt_tok, modulation(n, 0), MUL))

            def shift(n):
                tt(xt_tok, xt_tok, modulation(n, 1), ADD).then_inc(xt_done, 1)

            c = Chain(pool, pool_prep)
            pool.wait_ge(tables_ready, 1)
            pool.memset(zt[:, :, :].rearrange("p i m -> p (i m)"), 0.0).then_inc(zt_zero, 1)
            pool.wait_ge(c_sb, 1)
            powers_of_c(c, 0, cpow[0])
            pool.wait_ge(rows_in, 32)
            for b in range(D // UN):
                pool.wait_ge(ada1_sb, 2 * b + 2)
                sc, sh = sb[:, 0, b * UN:(b + 1) * UN], sb[:, 1, b * UN:(b + 1) * UN]
                c(tt(sc, sc, bmod_row[:, D + b * UN:D + (b + 1) * UN], ADD))
                c.settle()
                c(pool.tensor_scalar(sc, sc, 1.0, None, ADD))
                c.settle()
                c(tt(sc, sc, gain_row[:, b * UN:(b + 1) * UN], MUL))
                c.settle()
                tt(sh, sh, bmod_row[:, b * UN:(b + 1) * UN], ADD).then_inc(mod_ready, 1)
            pool.wait_ge(mod_ready, D // UN)
            c = Chain(pool, pool_step)
            scale(c, 0)
            c.settle()
            shift(0)
            pool.wait_ge(c_sb, 2)
            powers_of_c(c, 1, cpow[1])
            first, tile_steps = c.n, 6

            def tile(k, b, left, before):
                c = Chain(pool, pool_step, first + k * tile_steps)
                if left >= 1:
                    scale(c, k + 1)
                    c.settle()
                    shift(k + 1)
                if left >= 2:
                    pool.wait_ge(c_sb, k + 3)
                    pool.wait_ge(y_done, k + 1)
                    powers_of_c(c, k + 2, cpow[b])
                    assert c.n == tile_steps, c.n

            s5_loop(pool, tile)
            GEMM_POOL(pool)


def kernel(**inputs):
    from concourse.bacc import Bacc
    from concourse.bass_utils import run_bass_kernel_spmd

    arrays = {name: value for name, value in inputs.items() if value.size}
    arrays.update(c_main=main_consts(), c_s5=s5_consts(), c_dft=dft_tables())
    nc = Bacc("TRN2", target_bir_lowering=False, num_devices=1)
    a = {name: nc.dram_tensor(f"in_{name}_dram", value.shape, mybir.dt.from_np(value.dtype), kind="ExternalInput").ap()
         for name, value in arrays.items()}
    out = nc.dram_tensor("out_0_dram", (1, TOK, D), F32, kind="ExternalOutput").ap()
    two_layer_kernel(nc, a, out)
    r = run_bass_kernel_spmd(nc, [{f"in_{name}_dram": value for name, value in arrays.items()}], core_ids=[0])
    return r.results[0]["out_0_dram"]
```
